# Optimizing a Trainium2 kernel written in Bass

```python
import jax, jax.numpy as jnp
from jax import lax
import numpy as np
import math
import jax
import jax.numpy as jnp

D_MODEL = 1024
BATCH = 1
SEQ = 256
DEPTH = 1

GRID_W = 64
CTX_LEN = 256
N_HEADS = 6
QK_NOPE_DIM = 128
QK_ROPE_DIM = 64
V_HEAD_DIM = 128
Q_LORA_RANK = 384
KV_LORA_RANK = 256
MLA_WIDTH = N_HEADS * V_HEAD_DIM
FOURIER_GROUPS = 4
FOURIER_GROUP_DIM = 64
FOURIER_WIDTH = FOURIER_GROUPS * FOURIER_GROUP_DIM
MIX_WIDTH = MLA_WIDTH + FOURIER_WIDTH
IN_PROJ_WIDTH = FOURIER_WIDTH + Q_LORA_RANK + KV_LORA_RANK + QK_ROPE_DIM
ROPE_BASE = 10000.0
Q_BLOCK = 128
N_EXPERTS = 32
TOP_K = 4
D_FF = 1024
SWIGLU_LIMIT = 7.0
SWIGLU_ALPHA = 1.702
EXPERT_BLOCK = 128
RMS_EPS = 1e-6
N_MOD = 6


def rms_norm(x, g):
    xf = x.astype(jnp.float32)
    y = xf * lax.rsqrt(jnp.mean(xf * xf, axis=-1, keepdims=True) + RMS_EPS)
    return (y * g.astype(jnp.float32)).astype(x.dtype)

def modulate(x, g, shift, scale):
    return rms_norm(x, g) * (1 + scale) + shift

def axial_rope_tables(n_tokens):
    rows = n_tokens // GRID_W
    row = jnp.repeat(jnp.arange(rows, dtype=jnp.float32), GRID_W)
    col = jnp.tile(jnp.arange(GRID_W, dtype=jnp.float32), rows)
    half = QK_ROPE_DIM // 2
    inv = 1.0 / (ROPE_BASE ** (jnp.arange(0, half, 2, dtype=jnp.float32) / half))
    ang = jnp.concatenate([row[:, None] * inv, col[:, None] * inv], axis=-1)
    return jnp.cos(ang), jnp.sin(ang)

def rotate(x, cos, sin):
    xf = x.astype(jnp.float32)
    xe, xo = xf[..., 0::2], xf[..., 1::2]
    out = jnp.stack([xe * cos - xo * sin, xe * sin + xo * cos], axis=-1)
    return out.reshape(x.shape).astype(x.dtype)

def mla_project(p, norm_q, norm_kv, w_q_up, w_kv_up, rope):
    B, N, _ = p.shape
    q_lat, kv_lat, k_rope = jnp.split(p, [Q_LORA_RANK, Q_LORA_RANK + KV_LORA_RANK], axis=-1)
    q = (rms_norm(q_lat, norm_q) @ w_q_up).reshape(B, N, N_HEADS, QK_NOPE_DIM + QK_ROPE_DIM)
    kv = (rms_norm(kv_lat, norm_kv) @ w_kv_up).reshape(B, N, N_HEADS, QK_NOPE_DIM + V_HEAD_DIM)
    q_nope, q_rope = jnp.split(q, [QK_NOPE_DIM], axis=-1)
    k_nope, v = jnp.split(kv, [QK_NOPE_DIM], axis=-1)
    if rope is not None:
        cos, sin = rope
        q_rope = rotate(q_rope, cos[:, None, :], sin[:, None, :])
        k_rope = rotate(k_rope, cos, sin)
    k_rope = jnp.broadcast_to(k_rope[:, :, None, :], (B, N, N_HEADS, QK_ROPE_DIM))
    q = jnp.concatenate([q_nope, q_rope], axis=-1)
    k = jnp.concatenate([k_nope, k_rope], axis=-1)
    return q, k, v

def attend(q, k, v):
    B, N, H, Dq = q.shape
    nb = N // Q_BLOCK
    scale = Dq ** -0.5
    qb = jnp.moveaxis(q.reshape(B, nb, Q_BLOCK, H, Dq), 1, 0)

    def one_block(q_blk):
        s = jnp.einsum('bqhd,bkhd->bhqk', q_blk, k, preferred_element_type=jnp.float32) * scale
        pr = jax.nn.softmax(s, axis=-1).astype(v.dtype)
        return jnp.einsum('bhqk,bkhd->bqhd', pr, v)

    o = lax.map(one_block, qb)
    return jnp.moveaxis(o, 0, 1).reshape(B, N, H * V_HEAD_DIM)

def fourier_mix(u, w):
    B, N, _ = u.shape
    ug = u.reshape(B, N, FOURIER_GROUPS, FOURIER_GROUP_DIM).astype(jnp.float32)
    f = jnp.fft.fft2(ug, axes=(1, 3), norm='ortho').real.astype(u.dtype)
    return jnp.einsum('bngc,gcd->bngd', f, w).reshape(B, N, FOURIER_WIDTH)

def moe(h, w_router, b_router, w_gate, b_gate, w_up, b_up, w_down, b_down):
    T, D = h.shape
    logits = jnp.dot(h, w_router, preferred_element_type=jnp.float32) + b_router.astype(jnp.float32)
    top_logit, top_idx = lax.top_k(logits, TOP_K)
    gates = jax.nn.softmax(top_logit, axis=-1)
    n_pairs = T * TOP_K
    flat_e = top_idx.reshape(n_pairs)
    order = jnp.argsort(flat_e)
    sorted_e = flat_e[order]
    pair_tok = order // TOP_K
    pair_gate = gates.reshape(n_pairs)[order].astype(h.dtype)
    counts = jnp.bincount(flat_e, length=N_EXPERTS)
    padded = (counts + EXPERT_BLOCK - 1) // EXPERT_BLOCK * EXPERT_BLOCK
    pad_end = jnp.cumsum(padded)
    pad_start = pad_end - padded
    start = jnp.cumsum(counts) - counts
    dest = pad_start[sorted_e] + jnp.arange(n_pairs) - start[sorted_e]
    n_blocks = -(-n_pairs // EXPERT_BLOCK) + N_EXPERTS
    slot_tok = jnp.zeros((n_blocks * EXPERT_BLOCK,), jnp.int32).at[dest].set(pair_tok.astype(jnp.int32))
    block_e = jnp.minimum(
        jnp.searchsorted(pad_end, jnp.arange(n_blocks) * EXPERT_BLOCK, side='right'), N_EXPERTS - 1)
    xs = h[slot_tok].reshape(n_blocks, EXPERT_BLOCK, D)

    def expert_block(args):
        xb, e = args
        g = jnp.minimum(xb @ w_gate[e] + b_gate[e], SWIGLU_LIMIT)
        u = jnp.clip(xb @ w_up[e] + b_up[e], -SWIGLU_LIMIT, SWIGLU_LIMIT)
        act = g * jax.nn.sigmoid(SWIGLU_ALPHA * g) * (u + 1)
        return act @ w_down[e] + b_down[e]

    ys = lax.map(expert_block, (xs, block_e)).reshape(n_blocks * EXPERT_BLOCK, D)
    y_pairs = ys[dest] * pair_gate[:, None]
    return jnp.zeros_like(h).at[pair_tok].add(y_pairs)

def first_inputs(seed: int = 0) -> dict:
    key = jax.random.key(seed)
    ks = jax.random.split(key, 32)
    f32 = jnp.float32
    L, D = DEPTH, D_MODEL

    def nrm(k, shape, scale):
        return jax.random.normal(k, shape, f32) * scale

    def gain(k, shape):
        return 1.0 + 0.05 * jax.random.normal(k, shape, f32)

    return {
        'x': nrm(ks[0], (BATCH, SEQ, D), 1.0),
        'c': nrm(ks[1], (BATCH, D), 1.0),
        'ctx': nrm(ks[2], (BATCH, CTX_LEN, D), 1.0),
        'c_ctx': nrm(ks[3], (D,), 1.0),
        'w_mod': nrm(ks[4], (L, D, N_MOD * D), 0.5 * D ** -0.5),
        'b_mod': nrm(ks[5], (L, N_MOD * D), 0.01),
        'norm_attn_pre': gain(ks[6], (L, D)),
        'norm_attn_post': gain(ks[7], (L, D)),
        'norm_ffn_pre': gain(ks[8], (L, D)),
        'norm_ffn_post': gain(ks[9], (L, D)),
        'w_in': nrm(ks[10], (L, D, IN_PROJ_WIDTH), D ** -0.5),
        'norm_q_lat': gain(ks[11], (L, Q_LORA_RANK)),
        'norm_kv_lat': gain(ks[12], (L, KV_LORA_RANK)),
        'w_q_up': nrm(ks[13], (L, Q_LORA_RANK, N_HEADS * (QK_NOPE_DIM + QK_ROPE_DIM)), Q_LORA_RANK ** -0.5),
        'w_kv_up': nrm(ks[14], (L, KV_LORA_RANK, N_HEADS * (QK_NOPE_DIM + V_HEAD_DIM)), KV_LORA_RANK ** -0.5),
        'w_fourier': nrm(ks[15], (L, FOURIER_GROUPS, FOURIER_GROUP_DIM, FOURIER_GROUP_DIM), FOURIER_GROUP_DIM ** -0.5),
        'w_out': nrm(ks[16], (L, MIX_WIDTH, D), MIX_WIDTH ** -0.5),
        'w_router': nrm(ks[17], (L, D, N_EXPERTS), D ** -0.5),
        'b_router': nrm(ks[18], (L, N_EXPERTS), 0.01),
        'w_gate': nrm(ks[19], (L, N_EXPERTS, D, D_FF), D ** -0.5),
        'b_gate': nrm(ks[20], (L, N_EXPERTS, D_FF), 0.01),
        'w_up': nrm(ks[21], (L, N_EXPERTS, D, D_FF), D ** -0.5),
        'b_up': nrm(ks[22], (L, N_EXPERTS, D_FF), 0.01),
        'w_down': nrm(ks[23], (L, N_EXPERTS, D_FF, D), D_FF ** -0.5),
        'b_down': nrm(ks[24], (L, N_EXPERTS, D), 0.01),
    }

def first_block(x, c, ctx, c_ctx, w_mod, b_mod, norm_attn_pre, norm_attn_post, norm_ffn_pre,
              norm_ffn_post, w_in, norm_q_lat, norm_kv_lat, w_q_up, w_kv_up, w_fourier, w_out,
              w_router, b_router, w_gate, b_gate, w_up, b_up, w_down, b_down):
    B, N, D = x.shape
    rope = axial_rope_tables(N)
    for l in range(DEPTH):
        last = l == DEPTH - 1
        m = jax.nn.silu(c) @ w_mod[l] + b_mod[l]
        sh1, sc1, g1, sh2, sc2, g2 = jnp.split(m[:, None, :], N_MOD, axis=-1)
        mc = jax.nn.silu(c_ctx) @ w_mod[l] + b_mod[l]
        csh1, csc1, cg1, csh2, csc2, cg2 = jnp.split(mc, N_MOD, axis=-1)

        hx = modulate(x, norm_attn_pre[l], sh1, sc1)
        hc = modulate(ctx, norm_attn_pre[l], csh1, csc1)
        px = hx @ w_in[l]
        pc = hc @ w_in[l]
        qx, kx, vx = mla_project(px[..., FOURIER_WIDTH:], norm_q_lat[l], norm_kv_lat[l],
                                 w_q_up[l], w_kv_up[l], rope)
        qc, kc, vc = mla_project(pc[..., FOURIER_WIDTH:], norm_q_lat[l], norm_kv_lat[l],
                                 w_q_up[l], w_kv_up[l], None)
        k_all = jnp.concatenate([kx, kc], axis=1)
        v_all = jnp.concatenate([vx, vc], axis=1)
        att_x = attend(qx, k_all, v_all)
        four_x = fourier_mix(px[..., :FOURIER_WIDTH], w_fourier[l])
        mix_x = jnp.concatenate([att_x, four_x], axis=-1) @ w_out[l]
        x = x + g1 * rms_norm(mix_x, norm_attn_post[l])
        if not last:
            att_c = attend(qc, kc, vc)
            four_c = fourier_mix(pc[..., :FOURIER_WIDTH], w_fourier[l])
            mix_c = jnp.concatenate([att_c, four_c], axis=-1) @ w_out[l]
            ctx = ctx + cg1 * rms_norm(mix_c, norm_attn_post[l])

        hx2 = modulate(x, norm_ffn_pre[l], sh2, sc2)
        yx = moe(hx2.reshape(B * N, D), w_router[l], b_router[l], w_gate[l], b_gate[l],
                 w_up[l], b_up[l], w_down[l], b_down[l]).reshape(B, N, D)
        x = x + g2 * rms_norm(yx, norm_ffn_post[l])
        if not last:
            hc2 = modulate(ctx, norm_ffn_pre[l], csh2, csc2)
            yc = moe(hc2.reshape(-1, D), w_router[l], b_router[l], w_gate[l], b_gate[l],
                     w_up[l], b_up[l], w_down[l], b_down[l]).reshape(ctx.shape)
            ctx = ctx + cg2 * rms_norm(yc, norm_ffn_post[l])
    return x


D_A = D_MODEL // 2
GMLP_GROUPS = 4
GMLP_CHUNK = 128
D_B = D_MODEL // 2
CONV_WIDTH = 31
HEAD_DIM = 64
N_HEADS_2 = D_MODEL // 128
D_C = N_HEADS_2 * HEAD_DIM
MOBA_BLOCK = 256
MOBA_TOPK = 3
Q_CHUNK = 128
N_BRANCH = 3
D_BRANCH = 512
W_IN_COLS = 3 * D_A + 3 * D_B + 4 * D_C + N_BRANCH * D_MODEL
ALPHA = (2 * DEPTH) ** 0.25
BETA = (8 * DEPTH) ** -0.25
LN_EPS = 1e-5


def layer_norm(x, g, b):
    xf = x.astype(jnp.float32)
    mu = jnp.mean(xf, axis=-1, keepdims=True)
    var = jnp.mean(jnp.square(xf - mu), axis=-1, keepdims=True)
    y = (xf - mu) * lax.rsqrt(var + LN_EPS)
    return (y * g + b).astype(x.dtype)

def gmlp_spatial(v, sg_w, sg_b):
    B, S, _ = v.shape
    nc = S // GMLP_CHUNK
    cg = D_A // GMLP_GROUPS
    mask = jnp.tril(jnp.ones((GMLP_CHUNK, GMLP_CHUNK), dtype=bool))
    wm = jnp.where(mask[None], sg_w, jnp.zeros_like(sg_w))
    vc = v.reshape(B, nc, GMLP_CHUNK, GMLP_GROUPS, cg)
    z = jnp.einsum('gts,bnsgc->bntgc', wm, vc) + sg_b.T[None, None, :, :, None]
    return z.reshape(B, S, D_A)

def causal_depthwise_conv(x, w, b):
    C = x.shape[-1]
    y = lax.conv_general_dilated(
        x, w[:, None, :], window_strides=(1,), padding=[(CONV_WIDTH - 1, 0)],
        dimension_numbers=('NWC', 'WIO', 'NWC'), feature_group_count=C)
    return y + b

def moba_attention(q, k, v):
    B, S, H, Dh = q.shape
    nb = -(-S // MOBA_BLOCK)
    pad = nb * MOBA_BLOCK - S
    topk = min(MOBA_TOPK, nb)
    q = q.transpose(0, 2, 1, 3)
    k = jnp.pad(k.transpose(0, 2, 1, 3), ((0, 0), (0, 0), (0, pad), (0, 0)))
    v = jnp.pad(v.transpose(0, 2, 1, 3), ((0, 0), (0, 0), (0, pad), (0, 0)))
    kb = k.reshape(B, H, nb, MOBA_BLOCK, Dh)
    vb = v.reshape(B, H, nb, MOBA_BLOCK, Dh)
    kmean = jnp.mean(kb.astype(jnp.float32), axis=3)
    gate = jnp.einsum('bhsd,bhnd->bhsn', q.astype(jnp.float32), kmean)
    q_blk = jnp.arange(S) // MOBA_BLOCK
    past = jnp.arange(nb)[None, :] < q_blk[:, None]
    gate = jnp.where(past[None, None], gate, -jnp.inf)
    _, sel = lax.top_k(gate, topk)

    nq = S // Q_CHUNK
    q_c = q.reshape(B, H, nq, Q_CHUNK, Dh).transpose(2, 0, 1, 3, 4)
    sel_c = sel.reshape(B, H, nq, Q_CHUNK, topk).transpose(2, 0, 1, 3, 4)
    slopes = 2.0 ** (-(jnp.arange(1, H + 1, dtype=jnp.float32) * 8.0 / H))
    scale = Dh ** -0.5
    bi = jnp.arange(B)[:, None, None, None]
    hi = jnp.arange(H)[None, :, None, None]
    kpos = jnp.arange(MOBA_BLOCK)

    def one_chunk(args):
        qc, selc, c = args
        t = c * Q_CHUNK + jnp.arange(Q_CHUNK)
        blk = (c * Q_CHUNK) // MOBA_BLOCK
        kg = kb[bi, hi, selc]
        vg = vb[bi, hi, selc]
        lp = jnp.einsum('bhqd,bhqnkd->bhqnk', qc, kg).astype(jnp.float32) * scale
        spos = selc[..., None] * MOBA_BLOCK + kpos
        dist_p = (t[None, None, :, None, None] - spos).astype(jnp.float32)
        lp = lp - slopes[None, :, None, None, None] * dist_p
        valid = (jnp.arange(topk) < blk)[None, None, None, :, None]
        lp = jnp.where(valid, lp, -jnp.inf).reshape(B, H, Q_CHUNK, topk * MOBA_BLOCK)
        ko = lax.dynamic_index_in_dim(kb, blk, axis=2, keepdims=False)
        vo = lax.dynamic_index_in_dim(vb, blk, axis=2, keepdims=False)
        lo = jnp.einsum('bhqd,bhkd->bhqk', qc, ko).astype(jnp.float32) * scale
        dist_o = t[:, None] - (blk * MOBA_BLOCK + kpos)[None, :]
        lo = jnp.where(dist_o[None, None] >= 0,
                       lo - slopes[None, :, None, None] * dist_o.astype(jnp.float32)[None, None],
                       -jnp.inf)
        p = jax.nn.softmax(jnp.concatenate([lp, lo], axis=-1), axis=-1).astype(vb.dtype)
        out = jnp.einsum('bhqn,bhqnd->bhqd', p[..., :topk * MOBA_BLOCK],
                         vg.reshape(B, H, Q_CHUNK, topk * MOBA_BLOCK, Dh))
        out = out + jnp.einsum('bhqk,bhkd->bhqd', p[..., topk * MOBA_BLOCK:], vo)
        return out

    out = lax.map(one_chunk, (q_c, sel_c, jnp.arange(nq)))
    return out.transpose(1, 0, 3, 2, 4).reshape(B, S, H * Dh)

def hybrid_layer(x, w_in, sg_w, sg_b, v_ln_g, v_ln_b, conv_w, conv_b, cv_ln_g, cv_ln_b,
                 w_branch, w_out, ln_g, ln_b):
    B, S, D = x.shape
    h = x @ w_in
    cuts = np.cumsum([D_A, D_A, D_A, D_B, D_B, D_B, D_C, D_C, D_C, D_C])
    (a_u, a_v, a_g, b_val, b_glu, b_g, c_q, c_k, c_v, c_g, merge) = jnp.split(h, cuts, axis=-1)
    y_a = a_u * gmlp_spatial(layer_norm(a_v, v_ln_g, v_ln_b), sg_w, sg_b)
    y_a = y_a * jax.nn.silu(a_g)
    glu = b_val * jax.nn.sigmoid(b_glu)
    cv = jax.nn.silu(layer_norm(causal_depthwise_conv(glu, conv_w, conv_b), cv_ln_g, cv_ln_b))
    y_b = cv * jax.nn.silu(b_g)
    att = moba_attention(c_q.reshape(B, S, N_HEADS_2, HEAD_DIM),
                         c_k.reshape(B, S, N_HEADS_2, HEAD_DIM),
                         c_v.reshape(B, S, N_HEADS_2, HEAD_DIM))
    y_c = att * jax.nn.silu(c_g)
    ys = jnp.stack([y_a, y_b, y_c], axis=2)
    branch = jnp.einsum('bsnc,ncd->bsnd', ys, w_branch)
    gates = jax.nn.sigmoid(merge.reshape(B, S, N_BRANCH, D))
    mixed = jnp.sum(gates * branch, axis=2)
    out = mixed @ w_out
    return layer_norm(ALPHA * x + out, ln_g, ln_b)

def second_inputs(seed: int = 0) -> dict:
    key = jax.random.key(seed)
    ks = jax.random.split(key, 16)
    f32 = jnp.float32
    cg_t = GMLP_CHUNK
    return {
        "x": jax.random.normal(ks[0], (BATCH, SEQ, D_MODEL), f32),
        "w_in": jax.random.normal(ks[1], (DEPTH, D_MODEL, W_IN_COLS), f32) * D_MODEL ** -0.5,
        "sg_w": jax.random.normal(ks[2], (DEPTH, GMLP_GROUPS, cg_t, cg_t), f32) * cg_t ** -0.5,
        "sg_b": 1.0 + 0.01 * jax.random.normal(ks[3], (DEPTH, GMLP_GROUPS, cg_t), f32),
        "v_ln_g": 1.0 + 0.02 * jax.random.normal(ks[4], (DEPTH, D_A), f32),
        "v_ln_b": 0.02 * jax.random.normal(ks[5], (DEPTH, D_A), f32),
        "conv_w": jax.random.normal(ks[6], (DEPTH, CONV_WIDTH, D_B), f32) * CONV_WIDTH ** -0.5,
        "conv_b": 0.02 * jax.random.normal(ks[7], (DEPTH, D_B), f32),
        "cv_ln_g": 1.0 + 0.02 * jax.random.normal(ks[8], (DEPTH, D_B), f32),
        "cv_ln_b": 0.02 * jax.random.normal(ks[9], (DEPTH, D_B), f32),
        "w_branch": jax.random.normal(ks[10], (DEPTH, N_BRANCH, D_BRANCH, D_MODEL), f32) * (D_BRANCH ** -0.5) * BETA,
        "w_out": jax.random.normal(ks[11], (DEPTH, D_MODEL, D_MODEL), f32) * (D_MODEL ** -0.5) * BETA,
        "ln_g": 1.0 + 0.02 * jax.random.normal(ks[12], (DEPTH, D_MODEL), f32),
        "ln_b": 0.02 * jax.random.normal(ks[13], (DEPTH, D_MODEL), f32),
    }

def second_block(x, w_in, sg_w, sg_b, v_ln_g, v_ln_b, conv_w, conv_b, cv_ln_g, cv_ln_b,
              w_branch, w_out, ln_g, ln_b):
    for l in range(DEPTH):
        x = hybrid_layer(x, w_in[l], sg_w[l], sg_b[l], v_ln_g[l], v_ln_b[l], conv_w[l], conv_b[l],
                         cv_ln_g[l], cv_ln_b[l], w_branch[l], w_out[l], ln_g[l], ln_b[l])
    return x


_first_inputs = second_inputs


def second_inputs(seed=0):
    import zlib

    import numpy as np

    out = dict(_first_inputs(seed))
    spreads = {}
    factors = {'sg_b': 8.0,
     'v_ln_g': 8.0,
     'v_ln_b': 8.0,
     'conv_b': 8.0,
     'cv_ln_g': 8.0,
     'cv_ln_b': 8.0,
     'ln_g': 2.886,
     'ln_b': 2.747}
    for name, (base, spread) in spreads.items():
        noise = np.random.default_rng([zlib.crc32(name.encode()), seed]).standard_normal(out[name].shape)
        drawn = base * np.exp(spread * noise) if base else spread * noise
        out[name] = jnp.asarray(drawn.astype(out[name].dtype))
    for name, factor in factors.items():
        out[name] = (out[name] * factor).astype(out[name].dtype)
    return out


_narrow_inputs = second_inputs


def second_inputs(seed=0):

    out = dict(_narrow_inputs(seed))
    wider = {'sg_b': 12.0,
     'v_ln_g': 9.47,
     'v_ln_b': 8.46,
     'cv_ln_g': 8.6,
     'cv_ln_b': 8.63,
     'ln_g': 3.24,
     'ln_b': 3.25}
    for name, times in wider.items():
        mean = out[name].mean()
        out[name] = (mean + times * (out[name] - mean)).astype(out[name].dtype)
    return out


DEPTH_3 = 2

N_MIXERS = 4
D_FF_3 = 2816
N_MOD_3 = 9
EPS = 1e-6

POOL_WINDOWS = (2, 4, 8, 16)
N_POOL = len(POOL_WINDOWS)
POOL_GROUP = D_MODEL // N_POOL

DIFF_HEADS = 8
DIFF_HEAD_DIM = D_MODEL // DIFF_HEADS // 2
DIFF_V_DIM = 2 * DIFF_HEAD_DIM
ROPE_THETA = 500000.0
ROT_DIM = DIFF_HEAD_DIM // 4

GQA_HEADS = 8
GQA_KV_HEADS = 2
GQA_HEAD_DIM = D_MODEL // GQA_HEADS
GQA_GROUP = GQA_HEADS // GQA_KV_HEADS
GQA_Q_DIM = GQA_HEADS * GQA_HEAD_DIM
GQA_KV_DIM = GQA_KV_HEADS * GQA_HEAD_DIM
AXIAL_THETA = 10000.0
AXIAL_DIM = GQA_HEAD_DIM // 2

CONV_WIDTH_3 = 3


def rms_norm_3(x, g):
    xf = x.astype(jnp.float32)
    y = xf * lax.rsqrt(jnp.mean(xf * xf, axis=-1, keepdims=True) + EPS)
    return (y * g.astype(jnp.float32)).astype(x.dtype)

def modulate_3(h, shift, scale):
    return h * (1 + scale) + shift

def swiglu(h, w_gu, w_down):
    g, u = jnp.split(h @ w_gu, 2, axis=-1)
    return (jax.nn.silu(g) * u) @ w_down

def rope_tables(pos, dim, theta):
    inv = 1.0 / (theta ** (jnp.arange(0, dim, 2, dtype=jnp.float32) / dim))
    ang = pos.astype(jnp.float32)[:, None] * inv[None, :]
    return jnp.cos(ang), jnp.sin(ang)

def rope(x, cos, sin):
    half = x.shape[-1] // 2
    xf = x.astype(jnp.float32)
    x1, x2 = xf[..., :half], xf[..., half:]
    c = cos[None, :, None, :]
    s = sin[None, :, None, :]
    return jnp.concatenate([x1 * c - x2 * s, x2 * c + x1 * s], axis=-1).astype(x.dtype)

def sweep_query_blocks(fn, q):
    b, s = q.shape[:2]
    nblk = s // Q_BLOCK
    qb = jnp.moveaxis(q.reshape((b, nblk, Q_BLOCK) + q.shape[2:]), 1, 0)
    out = jnp.moveaxis(lax.map(fn, qb), 0, 1)
    return out.reshape((b, s) + out.shape[3:])

def pool_mixer(h, pool_w, pool_scale):
    b, s, d = h.shape
    cs = jnp.concatenate([jnp.zeros((b, 1, d), jnp.float32),
                          jnp.cumsum(h.astype(jnp.float32), axis=1)], axis=1)
    t = jnp.arange(s)
    diffs = []
    for g, win in enumerate(POOL_WINDOWS):
        lo = jnp.clip(t - win // 2, 0, s)
        hi = jnp.clip(t + win // 2, 0, s)
        csg = cs[..., g * POOL_GROUP:(g + 1) * POOL_GROUP]
        mean = (jnp.take(csg, hi, axis=1) - jnp.take(csg, lo, axis=1)) / (hi - lo).astype(jnp.float32)[None, :, None]
        diffs.append(mean.astype(h.dtype) - h[..., g * POOL_GROUP:(g + 1) * POOL_GROUP])
    dgrp = jnp.stack(diffs, axis=2)
    y = jnp.einsum('bsgc,gce->bsge', dgrp, pool_w).reshape(b, s, d)
    return y * pool_scale

def diff_attention(h, w_qkv, lam, subln_g, w_o, cos, sin, layer_idx):
    b, s, d = h.shape
    q, k, v = jnp.split(h @ w_qkv, 3, axis=-1)
    q = q.reshape(b, s, 2 * DIFF_HEADS, DIFF_HEAD_DIM)
    k = k.reshape(b, s, 2 * DIFF_HEADS, DIFF_HEAD_DIM)
    v = v.reshape(b, s, DIFF_HEADS, DIFF_V_DIM)
    q = jnp.concatenate([rope(q[..., :ROT_DIM], cos, sin), q[..., ROT_DIM:]], axis=-1)
    k = jnp.concatenate([rope(k[..., :ROT_DIM], cos, sin), k[..., ROT_DIM:]], axis=-1)
    q = (q * DIFF_HEAD_DIM ** -0.5).reshape(b, s, DIFF_HEADS, 2, DIFF_HEAD_DIM)
    k = k.reshape(b, s, DIFF_HEADS, 2, DIFF_HEAD_DIM)
    lam_init = 0.8 - 0.6 * math.exp(-0.3 * layer_idx)
    lf = lam.astype(jnp.float32)
    lam_full = jnp.exp(jnp.sum(lf[0] * lf[1])) - jnp.exp(jnp.sum(lf[2] * lf[3])) + lam_init

    def block(qb):
        sc = jnp.einsum('bqhcd,bkhcd->bhcqk', qb, k, preferred_element_type=jnp.float32)
        p = jax.nn.softmax(sc, axis=-1)
        a = p[:, :, 0] - lam_full * p[:, :, 1]
        return jnp.einsum('bhqk,bkhe->bqhe', a.astype(v.dtype), v)

    o = sweep_query_blocks(block, q)
    o = rms_norm_3(o, subln_g) * (1 - lam_init)
    return o.reshape(b, s, d) @ w_o

def gqa_axial_attention(h, w_qkv, q_norm_g, k_norm_g, w_o, cos_r, sin_r, cos_c, sin_c):
    b, s, d = h.shape
    qkv = h @ w_qkv
    q = qkv[..., :GQA_Q_DIM].reshape(b, s, GQA_HEADS, GQA_HEAD_DIM)
    k = qkv[..., GQA_Q_DIM:GQA_Q_DIM + GQA_KV_DIM].reshape(b, s, GQA_KV_HEADS, GQA_HEAD_DIM)
    v = qkv[..., GQA_Q_DIM + GQA_KV_DIM:].reshape(b, s, GQA_KV_HEADS, GQA_HEAD_DIM)
    q = rms_norm_3(q, q_norm_g)
    k = rms_norm_3(k, k_norm_g)

    def axial(t):
        return jnp.concatenate([rope(t[..., :AXIAL_DIM], cos_r, sin_r),
                                rope(t[..., AXIAL_DIM:], cos_c, sin_c)], axis=-1)

    q = (axial(q) * GQA_HEAD_DIM ** -0.5).reshape(b, s, GQA_KV_HEADS, GQA_GROUP, GQA_HEAD_DIM)
    k = axial(k)

    def block(qb):
        sc = jnp.einsum('bqgrd,bkgd->bgrqk', qb, k, preferred_element_type=jnp.float32)
        p = jax.nn.softmax(sc, axis=-1)
        return jnp.einsum('bgrqk,bkgd->bqgrd', p.astype(v.dtype), v)

    o = sweep_query_blocks(block, q)
    return o.reshape(b, s, d) @ w_o

def short_conv_mixer(h, w_in, w_conv, w_out):
    d = h.shape[-1]
    gb, gc, u = jnp.split(h @ w_in, 3, axis=-1)
    z = gc * u
    zc = lax.conv_general_dilated(z, w_conv[:, None, :], window_strides=(1,),
                                  padding=[((CONV_WIDTH_3 - 1) // 2, (CONV_WIDTH_3 - 1) // 2)],
                                  dimension_numbers=('NWC', 'WIO', 'NWC'),
                                  feature_group_count=d)
    return (gb * zc) @ w_out

def third_inputs(seed: int = 0) -> dict:
    key = jax.random.key(seed)
    ks = jax.random.split(key, 24)

    def nrm(k, shape, scale):
        return jax.random.normal(k, shape, jnp.float32) * scale

    D = D_MODEL
    return {
        "x": nrm(ks[0], (BATCH, SEQ, D), 1.0),
        "c": nrm(ks[1], (BATCH, D), 1.0),
        "mod_w": nrm(ks[2], (DEPTH_3, D, N_MOD_3 * D), 0.5 * D ** -0.5),
        "mod_b": nrm(ks[3], (DEPTH_3, N_MOD_3 * D), 0.02),
        "norm_g": 1.0 + nrm(ks[4], (DEPTH_3, 3, D), 0.1),
        "ffn_w_gu": nrm(ks[5], (DEPTH_3, 2, D, 2 * D_FF_3), D ** -0.5),
        "ffn_w_down": nrm(ks[6], (DEPTH_3, 2, D_FF_3, D), D_FF_3 ** -0.5),
        "pool_w": nrm(ks[7], (N_POOL, POOL_GROUP, POOL_GROUP), POOL_GROUP ** -0.5),
        "pool_scale": 1.0 + nrm(ks[8], (D,), 0.1),
        "diff_w_qkv": nrm(ks[9], (D, 3 * D), D ** -0.5),
        "diff_lambda": nrm(ks[10], (4, DIFF_HEAD_DIM), 0.1),
        "diff_subln_g": 1.0 + nrm(ks[11], (DIFF_V_DIM,), 0.1),
        "diff_w_o": nrm(ks[12], (D, D), D ** -0.5),
        "gqa_w_qkv": nrm(ks[13], (D, GQA_Q_DIM + 2 * GQA_KV_DIM), D ** -0.5),
        "gqa_q_norm_g": 1.0 + nrm(ks[14], (GQA_HEAD_DIM,), 0.1),
        "gqa_k_norm_g": 1.0 + nrm(ks[15], (GQA_HEAD_DIM,), 0.1),
        "gqa_w_o": nrm(ks[16], (D, D), D ** -0.5),
        "conv_w_in": nrm(ks[17], (D, 3 * D), D ** -0.5),
        "conv_w": nrm(ks[18], (CONV_WIDTH_3, D), CONV_WIDTH_3 ** -0.5),
        "conv_w_out": nrm(ks[19], (D, D), D ** -0.5),
        "final_g": 1.0 + nrm(ks[20], (D,), 0.1),
    }

def third_block(x, c, mod_w, mod_b, norm_g, ffn_w_gu, ffn_w_down, pool_w, pool_scale,
              diff_w_qkv, diff_lambda, diff_subln_g, diff_w_o,
              gqa_w_qkv, gqa_q_norm_g, gqa_k_norm_g, gqa_w_o,
              conv_w_in, conv_w, conv_w_out, final_g):
    s = x.shape[1]
    t = jnp.arange(s)
    cos1, sin1 = rope_tables(t, ROT_DIM, ROPE_THETA)
    rows = s // GRID_W
    row_pos = jnp.broadcast_to(jnp.arange(rows)[:, None], (rows, GRID_W)).reshape(-1)
    col_pos = jnp.broadcast_to(jnp.arange(GRID_W)[None, :], (rows, GRID_W)).reshape(-1)
    cos_r, sin_r = rope_tables(row_pos, AXIAL_DIM, AXIAL_THETA)
    cos_c, sin_c = rope_tables(col_pos, AXIAL_DIM, AXIAL_THETA)

    c_act = jax.nn.silu(c)
    for i in range(DEPTH_3):
        mod = (c_act @ mod_w[i] + mod_b[i])[:, None, :]
        sh0, sc0, g0, sh1, sc1, g1, sh2, sc2, g2 = jnp.split(mod, N_MOD_3, axis=-1)

        h = modulate_3(rms_norm_3(x, norm_g[i, 0]), sh0, sc0)
        x = x + 0.5 * g0 * swiglu(h, ffn_w_gu[i, 0], ffn_w_down[i, 0])

        h = modulate_3(rms_norm_3(x, norm_g[i, 1]), sh1, sc1)
        kind = i % N_MIXERS
        if kind == 0:
            y = pool_mixer(h, pool_w, pool_scale)
        elif kind == 1:
            y = diff_attention(h, diff_w_qkv, diff_lambda, diff_subln_g, diff_w_o, cos1, sin1, i)
        elif kind == 2:
            y = gqa_axial_attention(h, gqa_w_qkv, gqa_q_norm_g, gqa_k_norm_g, gqa_w_o,
                                    cos_r, sin_r, cos_c, sin_c)
        else:
            y = short_conv_mixer(h, conv_w_in, conv_w, conv_w_out)
        x = x + g1 * y

        h = modulate_3(rms_norm_3(x, norm_g[i, 2]), sh2, sc2)
        x = x + 0.5 * g2 * swiglu(h, ffn_w_gu[i, 1], ffn_w_down[i, 1])

    return rms_norm_3(x, final_g)


def setup_inputs(seed=0):
    out = dict(first_inputs(seed))
    for name, value in second_inputs(seed + 1).items():
        if name != "x":
            out[name + "_2"] = value
    for name, value in third_inputs(seed + 2).items():
        if name != "x":
            out[name + "_3"] = value
    return out


def reference(
    x, c, ctx, c_ctx, w_mod, b_mod, norm_attn_pre, norm_attn_post, norm_ffn_pre, norm_ffn_post,
    w_in, norm_q_lat, norm_kv_lat, w_q_up, w_kv_up, w_fourier, w_out, w_router, b_router,
    w_gate, b_gate, w_up, b_up, w_down, b_down, w_in_2, sg_w_2, sg_b_2, v_ln_g_2, v_ln_b_2,
    conv_w_2, conv_b_2, cv_ln_g_2, cv_ln_b_2, w_branch_2, w_out_2, ln_g_2, ln_b_2, c_3, mod_w_3,
    mod_b_3, norm_g_3, ffn_w_gu_3, ffn_w_down_3, pool_w_3, pool_scale_3, diff_w_qkv_3,
    diff_lambda_3, diff_subln_g_3, diff_w_o_3, gqa_w_qkv_3, gqa_q_norm_g_3, gqa_k_norm_g_3,
    gqa_w_o_3, conv_w_in_3, conv_w_3, conv_w_out_3, final_g_3,
):
    x = first_block(
        x, c, ctx, c_ctx, w_mod, b_mod, norm_attn_pre, norm_attn_post, norm_ffn_pre,
        norm_ffn_post, w_in, norm_q_lat, norm_kv_lat, w_q_up, w_kv_up, w_fourier, w_out,
        w_router, b_router, w_gate, b_gate, w_up, b_up, w_down, b_down,
    )
    x = second_block(
        x, w_in_2, sg_w_2, sg_b_2, v_ln_g_2, v_ln_b_2, conv_w_2, conv_b_2, cv_ln_g_2, cv_ln_b_2,
        w_branch_2, w_out_2, ln_g_2, ln_b_2,
    )
    return third_block(
        x, c_3, mod_w_3, mod_b_3, norm_g_3, ffn_w_gu_3, ffn_w_down_3, pool_w_3, pool_scale_3,
        diff_w_qkv_3, diff_lambda_3, diff_subln_g_3, diff_w_o_3, gqa_w_qkv_3, gqa_q_norm_g_3,
        gqa_k_norm_g_3, gqa_w_o_3, conv_w_in_3, conv_w_3, conv_w_out_3, final_g_3,
    )


_drawn_inputs = setup_inputs


def setup_inputs(seed=0):
    import zlib

    import numpy as np

    out = dict(_drawn_inputs(seed))
    spreads = {}
    factors = {'norm_ffn_post': 2.742,
     'norm_q_lat': 6.343,
     'b_gate': 8.0,
     'b_up': 8.0,
     'b_down': 8.0,
     'mod_b_3': 5.453,
     'norm_g_3': 3.539,
     'pool_scale_3': 6.277,
     'diff_lambda_3': 8.0,
     'diff_subln_g_3': 7.573}
    for name, (base, spread) in spreads.items():
        noise = np.random.default_rng([zlib.crc32(name.encode()), seed]).standard_normal(out[name].shape)
        drawn = base * np.exp(spread * noise) if base else spread * noise
        out[name] = jnp.asarray(drawn.astype(out[name].dtype))
    for name, factor in factors.items():
        out[name] = (out[name] * factor).astype(out[name].dtype)
    return out
```

```python
from contextlib import ExitStack, contextmanager

import concourse.bass as bass
import numpy as np
from concourse import mybir

F32 = mybir.dt.float32
ALU = mybir.AluOpType
ACT = mybir.ActivationFunctionType
AX = mybir.AxisListType.X

P = 128
D = 1024
SEQ = 256
TT = SEQ // P
KT = D // P
RMS_EPS = 1e-6
LN_EPS = 1e-5
PIECE = 1024

H_MLA, NOPE, ROPE, VDIM = 6, 128, 64, 128
Q_RANK, KV_RANK, FOUR = 384, 256, 256
QT, KVT = Q_RANK // P, KV_RANK // P
W_IN1 = FOUR + Q_RANK + KV_RANK + ROPE
E, TOPK, DFF = 32, 4, 1024
LIMIT, SWISH = 7.0, 1.702

W2, D_A, CONV, H2, DH2 = 8192, 512, 31, 8, 64
ALPHA = 2.0 ** 0.25
LAYERS, DFF3, MODS3 = 2, 2816, 9
H3, DH3 = 8, 64
LAM_INIT = 0.8 - 0.6 * float(np.exp(-0.3))
WINDOWS = (2, 4, 8, 16)

TABLES = {"ident": 128, "cos1": 256, "sin1": 256, "turn1": 64, "dft_c": 512, "dft_s": 512, "group_c": 128,
          "group_s": 128, "upper": 128, "dist": 512, "count": 1024, "cos3": 256, "sin3": 256, "turn3": 128}
AT = dict(zip(TABLES, np.cumsum([0] + list(TABLES.values()))[:-1].tolist()))

VECTORS = [
    [("norm_attn_pre", 8), ("norm_ffn_pre", 8), ("norm_q_lat", 3), ("norm_kv_lat", 2), ("b_mod", 48)],
    [("conv_b_2", 4), ("cv_ln_g_2", 4), ("cv_ln_b_2", 4), ("norm_g_3", 48), ("diff_subln_g_3", 1)],
    [("mod_b_3", 144)], [("conv_w_2", 124)], [("b_gate", 256)], [("b_up", 256)],
]


class Signal:

    def __init__(self, nc, name, unit=1):
        self.sem, self.unit = nc.alloc_semaphore(name=name), unit
        self.sent, self.seen, self.turn, self.base = 0, {}, 0, 0

    def up(self):
        self.sent += self.unit
        return self.sem, self.unit

    def own(self, back=0):
        return self.sem, self.turn + (self.sent - back * self.unit)

    def next(self, eng, n=1):
        who = eng.engine
        self.seen[who] = self.seen.get(who, self.base) + n * self.unit
        return self.sem, self.turn + self.seen[who]

    def passed(self, eng, n):
        self.next(eng, n)

    def ahead(self, n=1):
        return self.sem, self.base + n * self.unit


@contextmanager
def turns(eng, count, *per_turn):
    with eng.Fori(0, count) as i:
        before = [(s.sent, s.seen.get(eng.engine, s.base)) for s, _ in per_turn]
        for s, n in per_turn:
            s.turn = i * (n * s.unit)
        yield i
        for (s, n), (sent, seen) in zip(per_turn, before):
            s.turn = 0
            dsent, dseen = s.sent - sent, s.seen.get(eng.engine, s.base) - seen
            assert dsent in (0, n * s.unit) and dseen in (0, n * s.unit) and dsent + dseen, (s.sem, dsent, dseen)
            if dsent:
                s.sent += (count - 1) * n * s.unit
            if dseen:
                s.seen[eng.engine] += (count - 1) * n * s.unit


class Core:

    def __init__(self, ctx, nc, ins, out):
        self.nc, self.ins, self.out = nc, ins, out
        self.bank = [ctx.enter_context(nc.psum_tensor(f"bank{b}", [P, 512], F32)) for b in range(8)]
        self.filled = [Signal(nc, f"filled{b}") for b in range(8)]
        self.emptied = [Signal(nc, f"emptied{b}") for b in range(8)]
        sb = lambda name, shape: ctx.enter_context(nc.sbuf_tensor(name, shape, F32))
        self.stage_signals = []
        self.x = sb("x", [P, TT, D])
        self.hT = sb("hT", [P, KT, SEQ])
        self.ident = sb("ident", [P, P])
        self.ones = sb("ones", [P, P])
        self.vec, n = {}, 0
        for group in VECTORS:
            for name, rows in group:
                self.vec[name] = n
                n += rows
        self.cols = sb("cols", [P, n])

    def clear_signals(self):
        self.nc.clear_and_free_semaphores([signal.sem for signal in self.stage_signals])
        self.stage_signals = []
        self.nc.all_engine_barrier()

    def column(self, name, at=0, n=1):
        a = self.vec[name] + at
        return self.cols[:, a:a + n]

    def claim(self, pe, b):
        if self.filled[b].sent:
            pe.wait_ge(self.emptied[b].sem, self.filled[b].turn + self.filled[b].sent)

    def read(self, eng, b):
        return self.emptied[b].sem, self.filled[b].turn + self.filled[b].seen[eng.engine]

    def copied(self, pe, *banks):
        for b in banks:
            pe.wait_ge(self.emptied[b].sem, self.filled[b].turn + self.filled[b].sent)


class Stage:

    def __init__(self, core, name):
        self.core, self.nc, self.name, self.ctx = core, core.nc, name, ExitStack()

    def __enter__(self):
        self.ctx.__enter__()
        for signal in self.core.filled + self.core.emptied:
            signal.base, signal.seen = signal.sent, {}
        return self

    def __exit__(self, *a):
        return self.ctx.__exit__(*a)

    def sb(self, name, shape):
        return self.ctx.enter_context(self.nc.sbuf_tensor(f"{self.name}_{name}", shape, F32))

    def sem(self, name, unit=1):
        signal = Signal(self.nc, f"{self.name}_{name}", unit)
        self.core.stage_signals.append(signal)
        return signal

    def landed(self, name):
        return self.sem(name, 16)

    def block(self):
        return self.ctx.enter_context(self.nc.Block())



def load_constants(core):
    nc, ins = core.nc, core.ins
    tab = ins["tables"]
    with Stage(core, "prep") as st:
        tiles = []
        for group in VECTORS:
            total, first = sum(r for _, r in group), core.vec[group[0][0]]
            for a in range(0, total, P):
                rows = min(P, total - a)
                tiles.append((st.sb(f"rows{len(tiles)}", [P, P]), st.landed(f"rows{len(tiles)}"), rows,
                              first + a, group, a))
        ident_in = st.landed("ident_in")
        ones_set = st.sem("ones_set")
        copied = st.sem("copied")
        block = st.block()

        @block.sync
        def _(sp):
            sp.dma_start(core.ident[:], tab[:, AT["ident"]:AT["ident"] + P]).then_inc(*ident_in.up())
            for tile, landed, rows, _, group, a in tiles:
                r = 0
                if len(group) == 1:
                    src = ins[group[0][0]]
                    sp.dma_start(tile[0:rows, :], src[a:a + rows, :]).then_inc(*landed.up())
                else:
                    for name, n in group:
                        sp.dma_start(tile[r:r + n, :], ins[name]).then_inc(*landed.up())
                        r += n

        @block.tensor
        def _(pe):
            pe.wait_ge(*ident_in.next(pe))
            for n, (tile, landed, rows, _, group, _) in enumerate(tiles):
                b = n % 4
                pe.wait_ge(*landed.next(pe, len(group)))
                core.claim(pe, b)
                nc.tensor.transpose(core.bank[b][:, 0:rows], tile[0:rows, :], core.ident[0:rows, 0:rows])\
                    .then_inc(*core.filled[b].up())

        @block.vector
        def _(dve):
            nc.vector.memset(core.ones[:], 1.0).then_inc(*ones_set.up())
            for n, (_, _, rows, first, _, _) in enumerate(tiles):
                b = n % 4
                dve.wait_ge(*core.filled[b].next(dve))
                nc.vector.tensor_copy(core.cols[:, first:first + rows], core.bank[b][:, 0:rows])\
                    .then_inc(*core.emptied[b].up())



def modulation(core, name, c, w, n_pieces, wanted, rows, bias, c2=None, wanted2=()):
    nc = core.nc
    with Stage(core, name) as st:
        n2 = 2 if c2 is not None else 0
        wbuf = [st.sb(f"w{s}", [P, KT, PIECE]) for s in range(2)]
        acc = st.sb("acc", [P, n_pieces * PIECE])
        acc2 = st.sb("acc2", [P, max(n2, 1) * PIECE])
        craw = st.sb("craw", [P, 2, KT])
        cact = st.sb("cact", [P, 2, KT])
        brow = st.sb("brow", [P, len(rows), PIECE])
        mrow = st.sb("mrow", [P, 2, PIECE])
        c_in, row_in = st.landed("c_in"), st.landed("row_in")
        w_in = [st.landed(f"w_in{s}") for s in range(2)]
        w_used = [st.sem(f"w_used{s}") for s in range(2)]
        c_ready, summed, step = st.sem("c_ready"), st.sem("summed"), st.sem("step")
        block = st.block()
        wv = w.rearrange("(p j) n -> p j n", j=KT)

        @block.sync
        def _(sp):
            sp.dma_start(craw[:, 0, :], c).then_inc(*c_in.up())
            if n2:
                sp.dma_start(craw[:, 1, :], c2).then_inc(*c_in.up())
            for s in range(2):
                sp.dma_start(wbuf[s][:], wv[:, :, s * PIECE:(s + 1) * PIECE]).then_inc(*w_in[s].up())
            for r, (_, b_dram, m, _) in enumerate(rows):
                sp.dma_start(brow[:, r, :], b_dram.partition_broadcast(P)).then_inc(*row_in.up())
                if not isinstance(m, float):
                    sp.dma_start(mrow[:, r, :], m.partition_broadcast(P)).then_inc(*row_in.up())
            with turns(sp, (n_pieces - 2) // 2, (w_used[0], 1), (w_used[1], 1), (w_in[0], 1), (w_in[1], 1)) as i:
                for s in range(2):
                    sp.wait_ge(*w_used[s].next(sp))
                    sp.dma_start(wbuf[s][:], wv[:, :, bass.ds(i * (2 * PIECE) + (2 + s) * PIECE, PIECE)])\
                        .then_inc(*w_in[s].up())
            if n_pieces % 2:
                sp.wait_ge(*w_used[0].next(sp))
                sp.dma_start(wbuf[0][:], wv[:, :, (n_pieces - 1) * PIECE:n_pieces * PIECE])\
                    .then_inc(*w_in[0].up())

        @block.scalar
        def _(act):
            act.wait_ge(*c_in.next(act, 2 if n2 else 1))
            for k in range(2 if n2 else 1):
                last = nc.scalar.activation(cact[:, k, :], craw[:, k, :], ACT.Silu)
            last.then_inc(*c_ready.up())

        @block.vector
        def _(dve):
            half = PIECE // 2

            def add_piece(s, dst, k, final):
                for j in range(KT):
                    for h in range(2):
                        o, src = dst(h * half, half), wbuf[s][:, j, h * half:(h + 1) * half]
                        if j == 0:
                            op = nc.vector.tensor_scalar(o, src, cact[:, k, 0:1], None, ALU.mult)
                        else:
                            dve.wait_ge(*step.own(1))
                            op = nc.vector.scalar_tensor_tensor(o, src, cact[:, k, j:j + 1], o, ALU.mult, ALU.add)
                        op.then_inc(*(w_used[s] if final and j == KT - 1 and h else step).up())

            def fixed(t, at):
                return lambda o, n: t[:, at + o:at + o + n]

            dve.wait_ge(*c_ready.next(dve))
            for s in range(2):
                dve.wait_ge(*w_in[s].next(dve))
                if n2:
                    add_piece(s, fixed(acc2, s * PIECE), 1, False)
                add_piece(s, fixed(acc, s * PIECE), 0, True)
            with turns(dve, (n_pieces - 2) // 2, (w_in[0], 1), (w_in[1], 1), (w_used[0], 1), (w_used[1], 1),
                       (step, 2 * (2 * KT - 1))) as i:
                for s in range(2):
                    dve.wait_ge(*w_in[s].next(dve))
                    add_piece(s, lambda o, n: acc[:, bass.ds(i * (2 * PIECE) + ((2 + s) * PIECE + o), n)], 0, True)
            if n_pieces % 2:
                dve.wait_ge(*w_in[0].next(dve))
                add_piece(0, fixed(acc, (n_pieces - 1) * PIECE), 0, True)
            dve.wait_ge(*w_used[(n_pieces - 1) % 2].own())
            nc.vector.tensor_copy(craw[:, 0, 0:1], cact[:, 0, 0:1]).then_inc(*summed.up())
            dve.wait_ge(*core.filled[0].next(dve))
            at = 0
            for piece, gain, dst in list(wanted) + list(wanted2):
                src = core.bank[0][:, at * KT:(at + 1) * KT]
                at += 1
                final = at == len(wanted) + len(wanted2)
                nc.vector.tensor_tensor(dst, src, bias(piece), ALU.add)\
                    .then_inc(*(core.emptied[0] if final else step).up())
                if gain is not None:
                    dve.wait_ge(*(core.read(dve, 0) if final else step.own()))
                    nc.vector.scalar_tensor_tensor(dst, dst, 1.0, gain, ALU.add, ALU.mult).then_inc(*step.up())
            dve.wait_ge(*row_in.next(dve, row_in.sent // 16))
            for r, (_, _, m, dst) in enumerate(rows):
                for h in range(2):
                    b = 1 + (2 * r + h) % 4
                    o = slice(h * 512, (h + 1) * 512)
                    dve.wait_ge(*core.filled[b].next(dve))
                    nc.vector.tensor_tensor(dst[:, o], core.bank[b][:], brow[:, r, o], ALU.add)\
                        .then_inc(*core.emptied[b].up())
                    dve.wait_ge(*core.read(dve, b))
                    if isinstance(m, float):
                        nc.vector.tensor_scalar(dst[:, o], dst[:, o], m, None, ALU.mult).then_inc(*step.up())
                    else:
                        nc.vector.tensor_tensor(dst[:, o], dst[:, o], mrow[:, r, o], ALU.mult).then_inc(*step.up())

        @block.tensor
        def _(pe):
            pe.wait_ge(*summed.next(pe))
            core.claim(pe, 0)
            at = 0
            for source, group in ((acc, wanted), (acc2, wanted2)):
                for piece, _, _ in group:
                    for j in range(KT):
                        a = piece * PIECE + j * P
                        last = nc.tensor.matmul(core.bank[0][:, at:at + 1], source[:, a:a + P], core.ones[:, 0:1],
                                                start=True, stop=True)
                        at += 1
            last.then_inc(*core.filled[0].up())
            for r, (piece, _, _, _) in enumerate(rows):
                for h in range(2):
                    b = 1 + (2 * r + h) % 4
                    core.claim(pe, b)
                    a = piece * PIECE + h * 512
                    nc.tensor.matmul(core.bank[b][:], core.ones[:], acc[:, a:a + 512], start=True, stop=True)\
                        .then_inc(*core.filled[b].up())



class Norm:

    def __init__(self, st, x, hT, scale=None, shift=None, tag=""):
        self.st, self.x, self.hT, self.scale, self.shift = st, x, hT, scale, shift
        self.sum_sq = st.sem(f"sum_sq{tag}")
        self.mean_sq = st.sem(f"mean_sq{tag}")
        self.root = st.sem(f"root{tag}")
        self.normed = st.sem(f"normed{tag}")
        self.inv = st.sem(f"inv{tag}")
        self.hT_dve, self.hT_act = st.sem(f"hT_dve{tag}"), st.sem(f"hT_act{tag}")
        if scale is not None:
            self.xn = st.sb(f"xn{tag}", [P, TT, D])
            self.small = st.sb(f"small{tag}", [P, 4 * TT])
        else:
            self.xn = x

    def scalar(self, act):
        nc, small = self.st.nc, self.scale is not None and self.small
        if self.scale is not None:
            for t in range(TT):
                nc.scalar.activation(self.xn[:, t, :], self.x[:, t, :], ACT.Square, accum_out=small[:, t:t + 1])\
                    .then_inc(*self.sum_sq.up())
            act.wait_ge(*self.mean_sq.next(act))
            nc.scalar.activation(small[:, 4:4 + TT], small[:, 2:2 + TT], ACT.Sqrt).then_inc(*self.root.up())
        core = self.st.core
        for j in (4, 5, 6, 7):
            b, o = j // 2, (j % 2) * SEQ
            if o == 0:
                act.wait_ge(*core.filled[b].next(act))
            src = core.bank[b][:, o:o + SEQ]
            if self.scale is None:
                op = nc.scalar.activation(self.hT[:, j, :], src, ACT.Copy)
            else:
                op = nc.scalar.activation(self.hT[:, j, :], src, ACT.Identity, scale=self.scale[:, j:j + 1],
                                          bias=self.shift[:, j:j + 1])
            op.then_inc(*(core.emptied[b] if o else self.hT_act).up())

    def vector(self, dve):
        nc, core = self.st.nc, self.st.core
        if self.scale is not None:
            small = self.small
            dve.wait_ge(*self.sum_sq.next(dve, TT))
            nc.vector.tensor_scalar(small[:, 2:2 + TT], small[:, 0:TT], 1.0 / D, RMS_EPS, ALU.mult, ALU.add)\
                .then_inc(*self.mean_sq.up())
            dve.wait_ge(*self.root.next(dve))
            nc.vector.reciprocal(small[:, 6:6 + TT], small[:, 4:4 + TT]).then_inc(*self.inv.up())
            dve.wait_ge(*self.inv.own())
            for t in range(TT):
                nc.vector.tensor_scalar(self.xn[:, t, :], self.x[:, t, :], small[:, 6 + t:7 + t], None, ALU.mult)\
                    .then_inc(*self.normed.up())
        for j in (0, 1, 2, 3):
            b, o = j // 2, (j % 2) * SEQ
            if o == 0:
                dve.wait_ge(*core.filled[b].next(dve))
            src = core.bank[b][:, o:o + SEQ]
            if self.scale is None:
                op = nc.vector.tensor_copy(self.hT[:, j, :], src)
            else:
                op = nc.vector.tensor_scalar(self.hT[:, j, :], src, self.scale[:, j:j + 1], self.shift[:, j:j + 1],
                                             ALU.mult, ALU.add)
            op.then_inc(*(core.emptied[b] if o else self.hT_dve).up())

    def tensor(self, pe):
        nc, core = self.st.nc, self.st.core
        if self.scale is not None:
            pe.wait_ge(*self.normed.next(pe, TT))
        for b in range(4):
            core.claim(pe, b)
            for h in range(2):
                for t in range(TT):
                    j = 2 * b + h
                    last = nc.tensor.transpose(core.bank[b][:, h * SEQ + t * P:h * SEQ + (t + 1) * P],
                                               self.xn[:, t, j * P:(j + 1) * P], core.ident[:])
            last.then_inc(*core.filled[b].up())
        core.copied(pe, 0, 1, 2, 3)


def rms_residual(st, act, dve, banks, row, y, junk, small, sig):
    nc, core = st.nc, st.core
    taken, mean, root, inv, step = sig
    if act is not None:
        for t in range(TT):
            for n in range(2 if banks else 0):
                b = banks[2 * t + n]
                act.wait_ge(*core.filled[b].next(act))
                nc.scalar.activation(y[:, t, n * 512:(n + 1) * 512], core.bank[b][:], ACT.Copy)\
                    .then_inc(*core.emptied[b].up())
                act.wait_ge(*core.read(act, b))
            nc.scalar.activation(junk[:, t, :], y[:, t, :], ACT.Square, accum_out=small[:, t:t + 1])\
                .then_inc(*taken.up())
        act.wait_ge(*mean.next(act))
        nc.scalar.activation(small[:, 4:4 + TT], small[:, 2:2 + TT], ACT.Sqrt).then_inc(*root.up())
    else:
        dve.wait_ge(*taken.next(dve, TT))
        nc.vector.tensor_scalar(small[:, 2:2 + TT], small[:, 0:TT], 1.0 / D, RMS_EPS, ALU.mult, ALU.add)\
            .then_inc(*mean.up())
        dve.wait_ge(*root.next(dve))
        nc.vector.reciprocal(small[:, 6:6 + TT], small[:, 4:4 + TT]).then_inc(*inv.up())
        dve.wait_ge(*inv.own())
        for t in range(TT):
            nc.vector.scalar_tensor_tensor(y[:, t, :], y[:, t, :], small[:, 6 + t:7 + t], row, ALU.mult, ALU.mult)\
                .then_inc(*step.up())
            dve.wait_ge(*step.own())
            nc.vector.tensor_tensor(core.x[:, t, :], core.x[:, t, :], y[:, t, :], ALU.add).then_inc(*step.up())



def mla(core):
    nc, ins = core.nc, core.ins
    tab = ins["tables"]
    with Stage(core, "mla") as st:
        win = st.sb("win", [P, KT * D])
        w_in = win[:, 0:KT * W_IN1].rearrange("p (k n) -> p k n", n=W_IN1)
        w_out = win[:, :].rearrange("p (k n) -> p k n", n=D)
        wq = st.sb("wq", [P, QT, H_MLA * (NOPE + ROPE)])
        wkv = st.sb("wkv", [P, KVT, H_MLA * (NOPE + VDIM)])
        wf = st.sb("wf", [P, 2, P])
        tabs = st.sb("tabs", [P, AT["upper"] - AT["cos1"]])
        table = lambda name: tabs[:, AT[name] - AT["cos1"]:AT[name] - AT["cos1"] + TABLES[name]]
        ctx_x = st.sb("ctx_x", [P, TT, D])
        ctx_hT = st.sb("ctx_hT", [P, KT, SEQ])
        small_in, w_in_in = st.landed("small_in"), st.landed("w_in_in")

        with Stage(core, "mla_norm") as s0:
            x_in, ctx_in = s0.landed("x_in"), s0.landed("ctx_in")
            nx = Norm(s0, core.x, core.hT, core.mod1[:, 1, :], core.mod1[:, 0, :])
            nctx = Norm(s0, ctx_x, ctx_hT, core.mod1[:, 3, :], core.mod1[:, 2, :], "c")
            zeroed = s0.sem("zeroed")
            block = s0.block()

            @block.sync
            def _(sp):
                sp.dma_start(core.x[:], ins["x"]).then_inc(*x_in.up())
                sp.dma_start(ctx_x[:], ins["ctx"]).then_inc(*ctx_in.up())
                sp.dma_start(w_in, ins["w_in"].rearrange("(k p) n -> p k n", p=P)).then_inc(*w_in_in.up())
                sp.dma_start(tabs[:], tab[:, AT["cos1"]:AT["upper"]]).then_inc(*small_in.up())
                sp.dma_start(wq[:], ins["w_q_up"].rearrange("(k p) n -> p k n", p=P)).then_inc(*small_in.up())
                sp.dma_start(wkv[:], ins["w_kv_up"].rearrange("(k p) n -> p k n", p=P)).then_inc(*small_in.up())
                sp.wait_ge(*zeroed.next(sp))
                for g in range(4):
                    o = (g % 2) * 64
                    sp.dma_start(wf[o:o + 64, g // 2, o:o + 64], ins["w_fourier"][g]).then_inc(*small_in.up())

            @block.gpsimd
            def _(pool):
                nc.gpsimd.memset(wf[:], 0.0).then_inc(*zeroed.up())

            @block.scalar
            def _(act):
                act.wait_ge(*x_in.next(act))
                nx.scalar(act)
                act.wait_ge(*ctx_in.next(act))
                nctx.scalar(act)

            @block.vector
            def _(dve):
                dve.wait_ge(*x_in.next(dve))
                nx.vector(dve)
                dve.wait_ge(*ctx_in.next(dve))
                nctx.vector(dve)

            @block.tensor
            def _(pe):
                nx.tensor(pe)
                nctx.tensor(pe)

        with Stage(core, "mla_heads") as s1:
            px = s1.sb("px", [P, TT, FOUR + Q_RANK + KV_RANK])
            pc = s1.sb("pc", [P, TT, KV_RANK])
            kr = s1.sb("kr", [ROPE, 2 * SEQ])
            rot = s1.sb("rot", [ROPE, 2, SEQ])
            stat = s1.sb("stat", [P, 4 * 6])
            qlT = s1.sb("qlT", [P, QT, SEQ])
            kvT = s1.sb("kvT", [P, KVT, 2 * SEQ])
            v = s1.sb("v", [P, 2 * TT, H_MLA * VDIM])
            fa = s1.sb("fa", [P, 2, 2 * SEQ])
            ff = s1.sb("ff", [P, 2, SEQ])
            mixT = s1.sb("mixT", [P, KT, SEQ])
            kT = [s1.sb(f"kT{i}", [P, 2 * SEQ]) for i in range(2)]
            qT = [s1.sb(f"qT{i}", [P, SEQ]) for i in range(2)]
            qr = [s1.sb(f"qr{i}", [ROPE, SEQ]) for i in range(2)]
            prob = [s1.sb(f"prob{i}", [P, TT, 2 * SEQ]) for i in range(2)]
            probT = [s1.sb(f"probT{i}", [P, 2 * TT, SEQ]) for i in range(2)]
            soft = s1.sb("soft", [P, 4, H_MLA * TT])
            apost = ctx_hT[:].rearrange("p k n -> p (k n)")[:, 0:D]
            nsmall = s1.sb("nsmall", [P, 4 * TT])
            w_out_in, gain_in = s1.landed("w_out_in"), s1.landed("gain_in")
            kr_done = s1.sem("kr_done")
            lat_sq, lat_mean, lat_root, lat_inv = [s1.sem(f"lat_{n}") for n in ("sq", "mean", "root", "inv")]
            lat_done = s1.sem("lat_done")
            qr_raw, q_ready = s1.sem("qr_raw"), s1.sem("q_ready")
            top, normed = s1.sem("top"), s1.sem("normed")
            step = s1.sem("step")
            post = [s1.sem(f"post_{n}") for n in ("taken", "mean", "root", "inv", "step")]
            SC = float(NOPE + ROPE) ** -0.5

            def latents():
                for t in range(TT):
                    yield px[:, t, FOUR:FOUR + Q_RANK]
                for t in range(TT):
                    yield px[:, t, FOUR + Q_RANK:]
                for t in range(TT):
                    yield pc[:, t, :]

            block = s1.block()

            @block.sync
            def _(sp):
                sp.wait_ge(*core.filled[5].ahead(1))
                sp.dma_start(apost, ins["norm_attn_post"].partition_broadcast(P)).then_inc(*gain_in.up())
                sp.dma_start(w_out, ins["w_out"].rearrange("(k p) n -> p k n", p=P)).then_inc(*w_out_in.up())

            @block.tensor
            def _(pe):
                bank = core.bank
                pe.wait_ge(*w_in_in.next(pe))
                for t in range(TT):
                    for n in range(2):
                        b = 2 * t + n
                        core.claim(pe, b)
                        for k in range(KT):
                            last = nc.tensor.matmul(bank[b][:, 0:448], core.hT[:, k, t * P:(t + 1) * P],
                                                    w_in[:, k, n * 448:(n + 1) * 448], start=k == 0, stop=k == KT - 1)
                        last.then_inc(*core.filled[b].up())
                core.claim(pe, 4)
                for t in range(TT):
                    for k in range(KT):
                        last = nc.tensor.matmul(bank[4][:, t * 256:(t + 1) * 256], ctx_hT[:, k, t * P:(t + 1) * P],
                                                w_in[:, k, FOUR + Q_RANK:FOUR + Q_RANK + KV_RANK],
                                                start=k == 0, stop=k == KT - 1)
                last.then_inc(*core.filled[4].up())
                core.claim(pe, 5)
                for s, src in enumerate((core.hT, ctx_hT)):
                    for k in range(KT):
                        last = nc.tensor.matmul(bank[5][0:ROPE, s * SEQ:(s + 1) * SEQ], w_in[:, k, W_IN1 - ROPE:W_IN1],
                                                src[:, k, :], start=k == 0, stop=k == KT - 1)
                last.then_inc(*core.filled[5].up())
                pe.wait_ge(*small_in.next(pe, 7))
                core.copied(pe, 5)
                nc.tensor.matmul(bank[5][0:ROPE, 0:SEQ], table("turn1")[0:ROPE, :], kr[:, 0:SEQ],
                                 start=True, stop=True).then_inc(*core.filled[5].up())
                core.copied(pe, 0, 1, 2, 3, 4)
                for g in range(2):
                    core.claim(pe, 4)
                    for m, name in enumerate(("dft_c", "dft_s")):
                        for t in range(TT):
                            last = nc.tensor.matmul(bank[4][:, m * SEQ:(m + 1) * SEQ], px[:, t, g * P:(g + 1) * P],
                                                    table(name)[:, t * SEQ:(t + 1) * SEQ],
                                                    start=t == 0, stop=t == TT - 1)
                    last.then_inc(*core.filled[4].up())
                pe.wait_ge(*lat_done.next(pe, 6))
                for b, fs in ((6, (0, 1)), (7, (2,))):
                    core.claim(pe, b)
                    for i, f in enumerate(fs):
                        for t in range(TT):
                            a = FOUR + f * P
                            last = nc.tensor.transpose(bank[b][:, i * SEQ + t * P:i * SEQ + (t + 1) * P],
                                                       px[:, t, a:a + P], core.ident[:])
                    last.then_inc(*core.filled[b].up())
                for f in range(KVT):
                    core.claim(pe, f)
                    for t in range(2 * TT):
                        src = px[:, t, FOUR + Q_RANK + f * P:FOUR + Q_RANK + (f + 1) * P] if t < TT \
                            else pc[:, t - TT, f * P:(f + 1) * P]
                        last = nc.tensor.transpose(bank[f][:, t * P:(t + 1) * P], src, core.ident[:])
                    last.then_inc(*core.filled[f].up())
                core.copied(pe, 4)
                core.claim(pe, 4)
                for g in range(2):
                    for m, name in enumerate(("group_c", "group_s")):
                        last = nc.tensor.matmul(bank[4][:, g * SEQ:(g + 1) * SEQ], table(name),
                                                fa[:, g, m * SEQ:(m + 1) * SEQ], start=m == 0, stop=m == 1)
                last.then_inc(*core.filled[4].up())
                core.copied(pe, 0, 1, 6, 7)
                for t in range(2 * TT):
                    for n in range(2):
                        core.claim(pe, 2 + n)
                        for k in range(KVT):
                            heads = wkv[:, k, :].rearrange("p (h c) -> p h c", c=NOPE + VDIM)
                            last = nc.tensor.matmul(bank[2 + n][:, 0:3 * VDIM], kvT[:, k, t * P:(t + 1) * P],
                                                    heads[:, 3 * n:3 * n + 3, NOPE:], start=k == 0, stop=k == KVT - 1)
                        last.then_inc(*core.filled[2 + n].up())
                core.copied(pe, 4)
                core.claim(pe, 4)
                for g in range(2):
                    last = nc.tensor.matmul(bank[4][:, g * SEQ:(g + 1) * SEQ], wf[:, g, :], ff[:, g, :],
                                            start=True, stop=True)
                last.then_inc(*core.filled[4].up())

                def project(h):
                    core.claim(pe, 0)
                    for k in range(KVT):
                        a = h * (NOPE + VDIM)
                        last = nc.tensor.matmul(bank[0][:], wkv[:, k, a:a + NOPE], kvT[:, k, :],
                                                start=k == 0, stop=k == KVT - 1)
                    last.then_inc(*core.filled[0].up())
                    core.claim(pe, 1)
                    a = h * (NOPE + ROPE)
                    for k in range(QT):
                        nc.tensor.matmul(bank[1][:, 0:SEQ], wq[:, k, a:a + NOPE], qlT[:, k, :],
                                         start=k == 0, stop=k == QT - 1)
                    for k in range(QT):
                        last = nc.tensor.matmul(bank[1][0:ROPE, SEQ:2 * SEQ], wq[:, k, a + NOPE:a + NOPE + ROPE],
                                                qlT[:, k, :], start=k == 0, stop=k == QT - 1)
                    last.then_inc(*core.filled[1].up())
                    pe.wait_ge(*qr_raw.next(pe))
                    core.claim(pe, 2)
                    nc.tensor.matmul(bank[2][0:ROPE, 0:SEQ], table("turn1")[0:ROPE, :], rot[:, 0, :],
                                     start=True, stop=True).then_inc(*core.filled[2].up())

                def scores(h):
                    pe.wait_ge(*q_ready.next(pe))
                    core.copied(pe, 0)
                    if h == 0:
                        pe.wait_ge(*kr_done.next(pe))
                    for t in range(TT):
                        b = 3 + 2 * (h % 2) + t
                        core.claim(pe, b)
                        nc.tensor.matmul(bank[b][:], qT[h % 2][:, t * P:(t + 1) * P], kT[h % 2][:],
                                         start=True, stop=False)
                        nc.tensor.matmul(bank[b][:], qr[h % 2][:, t * P:(t + 1) * P], kr[:], start=False, stop=True)\
                            .then_inc(*core.filled[b].up())

                def attend(h):
                    for t in range(TT):
                        pe.wait_ge(*normed.next(pe))
                        core.claim(pe, 7)
                        for c in range(2 * TT):
                            last = nc.tensor.transpose(bank[7][:, c * P:(c + 1) * P],
                                                       prob[h % 2][:, t, c * P:(c + 1) * P], core.ident[:])
                        last.then_inc(*core.filled[7].up())
                    core.copied(pe, 7)
                    core.claim(pe, 2)
                    for c in range(2 * TT):
                        last = nc.tensor.matmul(bank[2][:, 0:SEQ], v[:, c, h * VDIM:(h + 1) * VDIM],
                                                probT[h % 2][:, c, :], start=c == 0, stop=c == 2 * TT - 1)
                    last.then_inc(*core.filled[2].up())

                project(0)
                scores(0)
                for h in range(H_MLA):
                    if h + 1 < H_MLA:
                        project(h + 1)
                        scores(h + 1)
                    attend(h)
                pe.wait_ge(*w_out_in.next(pe))
                core.copied(pe, 2, 4)
                for t in range(TT):
                    for n in range(2):
                        b = 3 + 2 * t + n
                        core.claim(pe, b)
                        for k in range(KT):
                            last = nc.tensor.matmul(bank[b][:], mixT[:, k, t * P:(t + 1) * P],
                                                    w_out[:, k, n * 512:(n + 1) * 512], start=k == 0, stop=k == KT - 1)
                        last.then_inc(*core.filled[b].up())

            @block.vector
            def _(dve):
                bank, cos, sin = core.bank, table("cos1")[0:ROPE, :], table("sin1")[0:ROPE, :]
                for b in (3, 5):
                    core.filled[b].passed(dve, 1)
                for t in range(TT):
                    dve.wait_ge(*core.filled[2 * t].next(dve))
                    nc.vector.tensor_copy(px[:, t, 0:448], bank[2 * t][:, 0:448])\
                        .then_inc(*core.emptied[2 * t].up())
                dve.wait_ge(*core.filled[4].next(dve))
                nc.vector.tensor_copy(pc[:], bank[4][:].rearrange("p (t n) -> p t n", t=TT))\
                    .then_inc(*core.emptied[4].up())
                dve.wait_ge(*lat_sq.next(dve, 6))
                nc.vector.tensor_scalar(stat[:, 6:8], stat[:, 0:2], 1.0 / Q_RANK, RMS_EPS, ALU.mult, ALU.add)\
                    .then_inc(*lat_mean.up())
                nc.vector.tensor_scalar(stat[:, 8:12], stat[:, 2:6], 1.0 / KV_RANK, RMS_EPS, ALU.mult, ALU.add)\
                    .then_inc(*lat_mean.up())
                dve.wait_ge(*lat_root.next(dve))
                nc.vector.reciprocal(stat[:, 18:24], stat[:, 12:18]).then_inc(*lat_inv.up())
                dve.wait_ge(*lat_inv.own())
                for i, part in enumerate(latents()):
                    nc.vector.tensor_scalar(part, part, stat[:, 18 + i:19 + i], None, ALU.mult)\
                        .then_inc(*lat_done.up())
                dve.wait_ge(*small_in.next(dve, 7))
                dve.wait_ge(*core.emptied[5].next(dve))
                dve.wait_ge(*core.filled[5].next(dve))
                nc.vector.tensor_tensor(rot[:, 1, :], bank[5][0:ROPE, 0:SEQ], sin, ALU.mult)\
                    .then_inc(*core.emptied[5].up())
                nc.vector.tensor_tensor(kr[:, 0:SEQ], kr[:, 0:SEQ], cos, ALU.mult).then_inc(*step.up())
                dve.wait_ge(*step.own())
                nc.vector.tensor_tensor(kr[:, 0:SEQ], kr[:, 0:SEQ], rot[:, 1, :], ALU.add).then_inc(*kr_done.up())
                for g in range(2):
                    dve.wait_ge(*core.filled[4].next(dve))
                    nc.vector.tensor_copy(fa[:, g, :], bank[4][:]).then_inc(*core.emptied[4].up())
                gain = core.column("norm_q_lat", 0, QT)
                for b, fs in ((6, (0, 1)), (7, (2,))):
                    dve.wait_ge(*core.filled[b].next(dve))
                    for i, f in enumerate(fs):
                        op = nc.vector.tensor_scalar(qlT[:, f, :], bank[b][:, i * SEQ:(i + 1) * SEQ],
                                                     gain[:, f:f + 1], None, ALU.mult)
                    op.then_inc(*core.emptied[b].up())
                dve.wait_ge(*core.filled[4].next(dve))
                nc.vector.tensor_copy(ff[:], bank[4][:].rearrange("p (g n) -> p g n", g=2))\
                    .then_inc(*core.emptied[4].up())
                for t in range(2 * TT):
                    dve.wait_ge(*core.filled[3].next(dve))
                    nc.vector.tensor_copy(v[:, t, 3 * VDIM:], bank[3][:, 0:3 * VDIM]).then_inc(*core.emptied[3].up())
                dve.wait_ge(*core.filled[4].next(dve))
                nc.vector.tensor_copy(mixT[:, H_MLA:, :], bank[4][:].rearrange("p (g n) -> p g n", g=2))\
                    .then_inc(*core.emptied[4].up())

                def rotate(h):
                    dve.wait_ge(*core.filled[1].next(dve))
                    nc.vector.tensor_copy(rot[:, 0, :], bank[1][0:ROPE, SEQ:2 * SEQ]).then_inc(*qr_raw.up())
                    nc.vector.tensor_copy(qT[h % 2][:], bank[1][:, 0:SEQ]).then_inc(*core.emptied[1].up())
                    dve.wait_ge(*qr_raw.own())
                    nc.vector.tensor_tensor(qr[h % 2][:], rot[:, 0, :], cos, ALU.mult).then_inc(*step.up())
                    dve.wait_ge(*core.filled[2].next(dve))
                    nc.vector.tensor_tensor(rot[:, 1, :], bank[2][0:ROPE, 0:SEQ], sin, ALU.mult)\
                        .then_inc(*core.emptied[2].up())
                    dve.wait_ge(*core.read(dve, 2))
                    nc.vector.tensor_tensor(qr[h % 2][:], qr[h % 2][:], rot[:, 1, :], ALU.add)\
                        .then_inc(*q_ready.up())

                def maxima(h):
                    for t in range(TT):
                        b, i = 3 + 2 * (h % 2) + t, h * TT + t
                        dve.wait_ge(*core.filled[b].next(dve))
                        nc.vector.reduce_max(soft[:, 0, i:i + 1], bank[b][:], AX).then_inc(*step.up())
                        dve.wait_ge(*step.own())
                        nc.vector.tensor_scalar(soft[:, 1, i:i + 1], soft[:, 0, i:i + 1], -SC, None, ALU.mult)\
                            .then_inc(*top.up())

                def finish(h):
                    for t in range(TT):
                        i = h * TT + t
                        dve.wait_ge(*core.emptied[3 + 2 * (h % 2) + t].next(dve))
                        nc.vector.reciprocal(soft[:, 3, i:i + 1], soft[:, 2, i:i + 1]).then_inc(*step.up())
                        dve.wait_ge(*step.own())
                        nc.vector.tensor_scalar(prob[h % 2][:, t, :], prob[h % 2][:, t, :], soft[:, 3, i:i + 1], None,
                                                ALU.mult).then_inc(*normed.up())
                    for t in range(TT):
                        dve.wait_ge(*core.filled[7].next(dve))
                        nc.vector.tensor_copy(probT[h % 2][:, :, t * P:(t + 1) * P],
                                              bank[7][:].rearrange("p (c n) -> p c n", c=2 * TT))\
                            .then_inc(*core.emptied[7].up())
                    dve.wait_ge(*core.filled[2].next(dve))
                    nc.vector.tensor_copy(mixT[:, h, :], bank[2][:, 0:SEQ]).then_inc(*core.emptied[2].up())

                for b, n in ((3, 5), (4, 5), (5, 1), (6, 1)):
                    core.emptied[b].passed(dve, n)
                core.filled[1].passed(dve, 2)
                core.filled[2].passed(dve, 4)
                rotate(0)
                maxima(0)
                for h in range(H_MLA):
                    if h + 1 < H_MLA:
                        rotate(h + 1)
                        maxima(h + 1)
                    finish(h)
                dve.wait_ge(*gain_in.next(dve))
                nc.vector.tensor_tensor(apost, apost, core.gate1[:, 0, :], ALU.mult).then_inc(*step.up())
                dve.wait_ge(*step.own())
                rms_residual(s1, None, dve, None, apost, core.hT[:].rearrange("p k n -> p (k n)")
                             .rearrange("p (t d) -> p t d", t=TT), None, nsmall, post)


            @block.scalar
            def _(act):
                bank = core.bank
                for t in range(TT):
                    b = 2 * t + 1
                    act.wait_ge(*core.filled[b].next(act))
                    nc.scalar.activation(px[:, t, 448:], bank[b][:, 0:448], ACT.Copy)\
                        .then_inc(*core.emptied[b].up())
                act.wait_ge(*core.filled[5].next(act))
                nc.scalar.activation(kr[:], bank[5][0:ROPE, :], ACT.Copy).then_inc(*core.emptied[5].up())
                for b in (0, 2, 4):
                    act.wait_ge(*core.emptied[b].next(act))
                act.wait_ge(*core.emptied[3].ahead(1))
                for i, part in enumerate(latents()):
                    junk = prob[0][:, i % 2, 0:part.shape[-1]]
                    if i >= 2:
                        act.wait_ge(*lat_sq.own(1))
                    nc.scalar.activation(junk, part, ACT.Square, accum_out=stat[:, i:i + 1]).then_inc(*lat_sq.up())
                act.wait_ge(*lat_mean.next(act, 2))
                nc.scalar.activation(stat[:, 12:18], stat[:, 6:12], ACT.Sqrt).then_inc(*lat_root.up())
                for b in (0, 2):
                    core.filled[b].passed(act, 1)
                gain = core.column("norm_kv_lat", 0, KVT)
                for f in range(KVT):
                    act.wait_ge(*core.filled[f].next(act))
                    nc.scalar.activation(kvT[:, f, :], bank[f][:], ACT.Identity, scale=gain[:, f:f + 1])\
                        .then_inc(*core.emptied[f].up())
                for t in range(2 * TT):
                    act.wait_ge(*core.filled[2].next(act))
                    nc.scalar.activation(v[:, t, 0:3 * VDIM], bank[2][:, 0:3 * VDIM], ACT.Copy)\
                        .then_inc(*core.emptied[2].up())

                def keys(h):
                    act.wait_ge(*core.filled[0].next(act))
                    nc.scalar.activation(kT[h % 2][:], bank[0][:], ACT.Copy).then_inc(*core.emptied[0].up())

                def exponents(h):
                    for t in range(TT):
                        b, i = 3 + 2 * (h % 2) + t, h * TT + t
                        act.wait_ge(*top.next(act))
                        nc.scalar.activation(prob[h % 2][:, t, :], bank[b][:], ACT.Exp, bias=soft[:, 1, i:i + 1],
                                             scale=SC, accum_out=soft[:, 2, i:i + 1])\
                            .then_inc(*core.emptied[b].up())

                keys(0)
                exponents(0)
                for h in range(1, H_MLA):
                    keys(h)
                    exponents(h)
                for b, n in ((3, 7), (4, 8), (5, 4), (6, 4)):
                    core.filled[b].passed(act, n)
                rms_residual(s1, act, None, (3, 4, 5, 6), None, core.hT[:].rearrange("p k n -> p (k n)")
                             .rearrange("p (t d) -> p t d", t=TT), ctx_x, nsmall, post)



def route(core, gates, gatesT):
    nc, ins = core.nc, core.ins
    with Stage(core, "route") as st:
        wr = st.sb("wr", [P, KT, E])
        br = st.sb("br", [P, E])
        w_in, b_in = st.landed("w_in"), st.landed("b_in")
        norm = Norm(st, core.x, core.hT, core.mod1[:, 5, :], core.mod1[:, 4, :])
        names = ("logit", "above", "equal", "rank", "mask", "expo")
        buf = {n: st.sb(n, [P, TT, E]) for n in names}
        top8 = st.sb("top8", [P, TT, 8])
        small = st.sb("stat", [P, 5, TT])
        step, shifted, exped, gated = [st.sem(n) for n in ("step", "shifted", "exped", "gated")]
        block = st.block()

        @block.sync
        def _(sp):
            sp.dma_start(wr[:], ins["w_router"].rearrange("(k p) n -> p k n", p=P)).then_inc(*w_in.up())
            sp.dma_start(br[:], ins["b_router"].partition_broadcast(P)).then_inc(*b_in.up())

        @block.tensor
        def _(pe):
            norm.tensor(pe)
            pe.wait_ge(*w_in.next(pe))
            core.claim(pe, 4)
            for t in range(TT):
                for k in range(KT):
                    last = nc.tensor.matmul(core.bank[4][:, t * E:(t + 1) * E], core.hT[:, k, t * P:(t + 1) * P],
                                            wr[:, k, :], start=k == 0, stop=k == KT - 1)
            last.then_inc(*core.filled[4].up())
            pe.wait_ge(*gated.next(pe, TT))
            core.claim(pe, 4)
            for t in range(TT):
                last = nc.tensor.transpose(core.bank[4][0:E, t * P:(t + 1) * P], gates[:, t, :], core.ident[:])
            last.then_inc(*core.filled[4].up())

        @block.scalar
        def _(act):
            norm.scalar(act)
            for t in range(TT):
                act.wait_ge(*shifted.next(act))
                nc.scalar.activation(buf["expo"][:, t, :], buf["rank"][:, t, :], ACT.Exp).then_inc(*exped.up())

        @block.vector
        def _(dve):
            vec = nc.vector

            def then(op, signal=step):
                op.then_inc(*signal.up())
                dve.wait_ge(*signal.own())

            norm.vector(dve)
            dve.wait_ge(*b_in.next(dve))
            dve.wait_ge(*core.filled[4].next(dve))
            for t in range(TT):
                op = vec.tensor_tensor(buf["logit"][:, t, :], core.bank[4][:, t * E:(t + 1) * E], br[:], ALU.add)
            op.then_inc(*core.emptied[4].up())
            dve.wait_ge(*core.read(dve, 4))
            for t in range(TT):
                logit, above, equal, rank, mask, expo = [buf[n][:, t, :] for n in names]
                then(vec.max(top8[:, t, :], logit))
                fourth = top8[:, t, TOPK - 1:TOPK]
                then(vec.tensor_scalar(above, logit, fourth, None, ALU.is_gt, ALU.add, accum_out=small[:, 0, t:t + 1]))
                then(vec.tensor_scalar(small[:, 1, t:t + 1], small[:, 0, t:t + 1], -1.0, float(TOPK), ALU.mult, ALU.add))
                then(vec.tensor_scalar(equal, logit, fourth, None, ALU.is_equal))
                then(vec.tensor_tensor_scan(rank, core.ones[:, 0:E], equal, 0.0, ALU.mult, ALU.add))
                then(vec.tensor_scalar(mask, rank, small[:, 1, t:t + 1], None, ALU.is_le))
                then(vec.tensor_tensor(mask, mask, equal, ALU.mult))
                then(vec.tensor_tensor(mask, mask, above, ALU.add))
                then(vec.tensor_scalar(rank, logit, top8[:, t, 0:1], None, ALU.subtract), shifted)
                dve.wait_ge(*exped.next(dve))
                then(vec.tensor_tensor(expo, expo, mask, ALU.mult))
                then(vec.reduce_sum(small[:, 2, t:t + 1], expo, AX))
                then(vec.reciprocal(small[:, 3, t:t + 1], small[:, 2, t:t + 1]))
                vec.tensor_scalar(gates[:, t, :], expo, small[:, 3, t:t + 1], None, ALU.mult).then_inc(*gated.up())
            dve.wait_ge(*core.filled[4].next(dve))
            vec.tensor_copy(gatesT[:], core.bank[4][0:E, 0:SEQ]).then_inc(*core.emptied[4].up())


def experts_dense(core, y, gates, gatesT):
    nc, ins = core.nc, core.ins
    with Stage(core, "dense") as st:
        part = [st.sb(f"part{u}", [P, 4096]) for u in range(6)]
        in_k = [part[u][:].rearrange("p (k n) -> p k n", k=KT) for u in range(4)]
        in_f = [part[u][:].rearrange("p (f n) -> p f n", f=4) for u in range(4, 6)]
        bd = st.sb("bd", [E, D])
        actT = st.sb("actT", [P, KT, SEQ])
        g = [st.sb(f"g{i}", [P, SEQ]) for i in range(2)]
        s = [st.sb(f"s{i}", [P, SEQ]) for i in range(2)]
        u_ = [st.sb(f"u{i}", [P, SEQ]) for i in range(2)]
        cur = st.sb("cur", [P, 2 * KT + TT])
        landed = [st.landed(f"part_in{u}") for u in range(6)]
        bd_in = st.landed("bd_in")
        g_ready, s_ready, act_ready, step = [st.sem(n) for n in ("g_ready", "s_ready", "act_ready", "step")]
        block = st.block()
        names = ("w_gate", "w_gate", "w_up", "w_up", "w_down", "w_down")

        def source(u, e):
            w = ins[names[u]]
            half = u % 2
            if u < 4:
                return w[e, :, half * 512:(half + 1) * 512].rearrange("o (k p) n -> p (o k) n", p=P)
            return w[e, half * 512:(half + 1) * 512, :].rearrange("o (f p) n -> p (o f) n", p=P)

        view = in_k + in_f

        @block.sync
        def _(sp):
            sp.dma_start(bd[:], ins["b_down"]).then_inc(*bd_in.up())
            for u in range(6):
                sp.dma_start(view[u], source(u, slice(0, 1))).then_inc(*landed[u].up())
            core.filled[3].passed(sp, 1)
            with turns(sp, E - 1, *[(x, 1) for x in landed], (core.filled[7], 2), (core.filled[3], 1)) as i:
                for parts, b in (((0, 2), 7), ((1, 3), 7), ((4, 5), 3)):
                    sp.wait_ge(*core.filled[b].next(sp))
                    for u in parts:
                        sp.dma_start(view[u], source(u, bass.ds(i + 1, 1))).then_inc(*landed[u].up())

        @block.tensor
        def _(pe):
            pe.wait_ge(*bd_in.next(pe))
            for t in range(TT):
                for n in range(2):
                    b = 2 * t + n
                    core.claim(pe, b)
                    nc.tensor.matmul(core.bank[b][:], gatesT[:, t * P:(t + 1) * P], bd[:, n * 512:(n + 1) * 512],
                                     start=True, stop=True).then_inc(*core.filled[b].up())
            with turns(pe, E, *[(x, 1) for x in landed], *[(core.filled[b], 1) for b in range(4)],
                       *[(core.filled[b], 2) for b in range(4, 8)], (act_ready, KT)) as _:
                for half in range(2):
                    pe.wait_ge(*landed[half].next(pe))
                    pe.wait_ge(*landed[2 + half].next(pe))
                    for f in range(4):
                        b = 4 + f
                        core.claim(pe, b)
                        for m in range(2):
                            w = in_k[2 * m + half]
                            for k in range(KT):
                                last = nc.tensor.matmul(core.bank[b][:, m * SEQ:(m + 1) * SEQ],
                                                        w[:, k, f * P:(f + 1) * P], core.hT[:, k, :],
                                                        start=k == 0, stop=k == KT - 1)
                        last.then_inc(*core.filled[b].up())
                for half in range(2):
                    pe.wait_ge(*landed[4 + half].next(pe))
                for t in range(TT):
                    for n in range(2):
                        b = 2 * t + n
                        core.claim(pe, b)
                        for f in range(KT):
                            if t == 0 and n == 0:
                                pe.wait_ge(*act_ready.next(pe))
                            last = nc.tensor.matmul(core.bank[b][:], actT[:, f, t * P:(t + 1) * P],
                                                    in_f[f // 4][:, f % 4, n * 512:(n + 1) * 512],
                                                    start=f == 0, stop=f == KT - 1)
                        last.then_inc(*core.filled[b].up())

        @block.scalar
        def _(act):
            with turns(act, E, (g_ready, KT), (s_ready, KT)):
                for f in range(KT):
                    act.wait_ge(*g_ready.next(act))
                    nc.scalar.activation(s[f % 2][:], g[f % 2][:], ACT.Sigmoid, scale=SWISH).then_inc(*s_ready.up())

        @block.vector
        def _(dve):
            vec = nc.vector
            for t in range(TT):
                for n in range(2):
                    b = 2 * t + n
                    dve.wait_ge(*core.filled[b].next(dve))
                    vec.tensor_copy(y[:, t, n * 512:(n + 1) * 512], core.bank[b][:]).then_inc(*core.emptied[b].up())
            with turns(dve, E, *[(core.filled[b], 1) for b in range(4)], *[(core.emptied[b], 1) for b in range(4)],
                       *[(core.filled[b], 2) for b in range(4, 8)], *[(core.emptied[b], 2) for b in range(4, 8)],
                       (g_ready, KT), (s_ready, KT), (act_ready, KT), (step, 3 + 2 * KT)) as e:
                vec.tensor_copy(cur[:, 0:KT], core.cols[:, bass.ds(e * KT + core.vec["b_gate"], KT)])\
                    .then_inc(*step.up())
                vec.tensor_copy(cur[:, KT:2 * KT], core.cols[:, bass.ds(e * KT + core.vec["b_up"], KT)])\
                    .then_inc(*step.up())
                vec.tensor_copy(cur[:, 2 * KT:], gates[:, :, bass.ds(e, 1)].rearrange("p t o -> p (t o)"))\
                    .then_inc(*step.up())
                dve.wait_ge(*step.own())
                for f in range(KT):
                    b, i = 4 + f % 4, f % 2
                    if f >= 2:
                        dve.wait_ge(*act_ready.own(1))
                    dve.wait_ge(*core.filled[b].next(dve))
                    vec.tensor_scalar(g[i][:], core.bank[b][:, 0:SEQ], cur[:, f:f + 1], LIMIT, ALU.add, ALU.min)\
                        .then_inc(*g_ready.up())
                    vec.tensor_scalar(u_[i][:], core.bank[b][:, SEQ:], cur[:, KT + f:KT + f + 1], LIMIT,
                                      ALU.add, ALU.min).then_inc(*core.emptied[b].up())
                    dve.wait_ge(*core.read(dve, b))
                    vec.tensor_scalar(u_[i][:], u_[i][:], -LIMIT, 1.0, ALU.max, ALU.add).then_inc(*step.up())
                    dve.wait_ge(*s_ready.next(dve))
                    vec.tensor_tensor(g[i][:], g[i][:], s[i][:], ALU.mult).then_inc(*step.up())
                    dve.wait_ge(*step.own())
                    vec.tensor_tensor(actT[:, f, :], g[i][:], u_[i][:], ALU.mult).then_inc(*act_ready.up())
                for t in range(TT):
                    for n in range(2):
                        b, o = 2 * t + n, slice(n * 512, (n + 1) * 512)
                        dve.wait_ge(*core.filled[b].next(dve))
                        vec.scalar_tensor_tensor(y[:, t, o], core.bank[b][:], cur[:, 2 * KT + t:2 * KT + t + 1],
                                                 y[:, t, o], ALU.mult, ALU.add).then_inc(*core.emptied[b].up())
                dve.wait_ge(*core.read(dve, 3))


def experts(core):
    nc, ins = core.nc, core.ins
    with Stage(core, "experts") as st:
        gates = st.sb("gates", [P, TT, E])
        gatesT = st.sb("gatesT", [E, SEQ])
        y = st.sb("y", [P, TT, D])
        route(core, gates, gatesT)
        experts_dense(core, y, gates, gatesT)
        with Stage(core, "experts_out") as s1:
            post = s1.sb("post", [P, D])
            junk = s1.sb("junk", [P, TT, D])
            small = s1.sb("small", [P, 4 * TT])
            gain_in, step = s1.landed("gain_in"), s1.sem("gain")
            sig = [s1.sem(f"post_{n}") for n in ("taken", "mean", "root", "inv", "step")]
            block = s1.block()

            @block.sync
            def _(sp):
                sp.dma_start(post[:], ins["norm_ffn_post"].partition_broadcast(P)).then_inc(*gain_in.up())

            @block.scalar
            def _(act):
                rms_residual(s1, act, None, None, None, y, junk, small, sig)

            @block.vector
            def _(dve):
                dve.wait_ge(*gain_in.next(dve))
                nc.vector.tensor_tensor(post[:], post[:], core.gate1[:, 1, :], ALU.mult).then_inc(*step.up())
                dve.wait_ge(*step.own())
                rms_residual(s1, None, dve, None, post[:], y, None, small, sig)



def second(core):
    nc, ins = core.nc, core.ins
    tab = ins["tables"]
    with Stage(core, "second") as st:
        pT = st.sb("pT", [P, W2 // P, SEQ])
        A_U, A_V, A_G, B_VAL, B_GLU, B_G, C_Q, C_K, C_V, C_G, MERGE = range(0, 44, 4)
        tiles = lambda a, n=4: pT[:, a:a + n, :]
        flat = lambda a: pT[:, a:a + 4, :].rearrange("p f n -> p (f n)")
        av = flat(A_V).rearrange("p (t n) -> p t n", t=TT)
        vtok = flat(C_V).rearrange("p (t n) -> p t n", t=TT)
        yT = [tiles(A_U), tiles(B_VAL), tiles(C_Q)]
        ring = st.sb("ring", [P, 2, 4096])
        w_k = [ring[:, s, :].rearrange("p (k n) -> p k n", k=KT) for s in range(2)]
        w_out = [ring[:, s, :].rearrange("p (k n) -> p k n", k=4) for s in range(2)]
        wb = st.sb("wb", [P, 3, 4, D])
        ln_rows = wb[:, 0, 0:2, :]
        rows = st.sb("rows", [P, 3, 512])
        upper = st.sb("upper", [P, P])
        dist = st.sb("dist", [P, TT * SEQ])
        sg = st.sb("sg", [P, 4, P])
        wmT = st.sb("wmT", [P, 4, P])
        glu = st.sb("glu", [P, 4, CONV - 1 + SEQ])
        logit = st.sb("logit", [P, H2, TT, SEQ])
        probT = [st.sb(f"probT{i}", [P, TT, SEQ]) for i in range(2)]
        tmp = st.sb("tmp", [P, 512])
        stat = st.sb("stat", [P, TT, 2, 6])
        aggr = st.sb("aggr", [P, TT, 6])
        soft = st.sb("soft", [P, 4, H2 * TT])
        chan = st.sb("chan", [P, 2, SEQ])
        mixedT = core.hT
        slot_in = [st.landed(f"slot_in{s}") for s in range(2)]
        consts_in, branch_in, out_in, ln_in = [st.landed(n) for n in ("consts_in", "branch_in", "out_in", "ln_in")]
        norm = Norm(st, core.x, core.hT)
        S = {n: st.sem(n) for n in ("padded", "sig_glu", "conv", "silu_a", "silu_b", "silu_c", "var", "dev",
                                       "av_ready", "step", "z_ready", "neg_top", "exped", "prob_ready",
                                       "centred", "squared", "chan_var", "chan_dev", "scaled", "cv_ready", "yb_ready",
                                       "mixed", "out_var", "out_dev")}
        slopes = [2.0 ** -(8.0 * (h + 1) / H2) for h in range(H2)]
        SC = DH2 ** -0.5
        block = st.block()
        w_in = ins["w_in_2"].rearrange("(k p) n -> p k n", p=P)

        @block.sync
        def _(sp):
            for s in range(2):
                sp.dma_start(w_k[s], w_in[:, :, s * 512:(s + 1) * 512]).then_inc(*slot_in[s].up())
            sp.dma_start(sg[:], ins["sg_w_2"].rearrange("g t s -> t g s")).then_inc(*consts_in.up())
            for i, name in enumerate(("v_ln_g_2", "v_ln_b_2", "sg_b_2")):
                sp.dma_start(rows[:, i, :], ins[name].partition_broadcast(P)).then_inc(*consts_in.up())
            sp.dma_start(upper[:], tab[:, AT["upper"]:AT["upper"] + P]).then_inc(*consts_in.up())
            sp.dma_start(dist[:], tab[:, AT["dist"]:AT["dist"] + 512]).then_inc(*consts_in.up())
            for b in (1, 3):
                core.filled[b].passed(sp, 1)
            with turns(sp, W2 // 1024 - 1, (slot_in[0], 1), (slot_in[1], 1), (core.filled[1], 1),
                       (core.filled[3], 1)) as i:
                for s in range(2):
                    sp.wait_ge(*core.filled[1 + 2 * s].next(sp))
                    sp.dma_start(w_k[s], w_in[:, :, bass.ds(i * 1024 + (1024 + s * 512), 512)])\
                        .then_inc(*slot_in[s].up())
            sp.dma_start(wb[:], ins["w_branch_2"].rearrange("b (k p) n -> p b k n", p=P)).then_inc(*branch_in.up())
            for s in range(2):
                sp.wait_ge(*core.filled[1 + 2 * s].next(sp))
                sp.dma_start(w_out[s], ins["w_out_2"][s * 512:(s + 1) * 512, :].rearrange("(k p) n -> p k n", p=P))\
                    .then_inc(*out_in.up())
            sp.wait_ge(*core.filled[7].ahead(6))
            for i, name in enumerate(("ln_g_2", "ln_b_2")):
                sp.dma_start(ln_rows[:, i, :], ins[name].partition_broadcast(P)).then_inc(*ln_in.up())

        @block.tensor
        def _(pe):
            bank = core.bank
            norm.tensor(pe)

            def project(count):
                with turns(pe, count, (slot_in[0], 1), (slot_in[1], 1), *[(core.filled[b], 1) for b in range(4)]):
                    for s in range(2):
                        pe.wait_ge(*slot_in[s].next(pe))
                        for q in range(2):
                            b = 2 * s + q
                            core.claim(pe, b)
                            for f in (2 * q, 2 * q + 1):
                                for k in range(KT):
                                    last = nc.tensor.matmul(bank[b][:, (f % 2) * SEQ:(f % 2 + 1) * SEQ],
                                                            w_k[s][:, k, f * P:(f + 1) * P], core.hT[:, k, :],
                                                            start=k == 0, stop=k == KT - 1)
                            last.then_inc(*core.filled[b].up())

            def values(h):
                b = 2 + h % 2
                core.copied(pe, h % 2)
                core.claim(pe, b)
                for c in range(TT):
                    last = nc.tensor.matmul(bank[b][:, 0:SEQ], vtok[:, c, (h // 2) * P:(h // 2 + 1) * P],
                                            probT[h % 2][:, c, :], start=c == 0, stop=c == TT - 1)
                last.then_inc(*core.filled[b].up())

            project(3)
            project(2)
            core.copied(pe, 0, 1, 2, 3)
            pe.wait_ge(*consts_in.next(pe, 6))
            for g in range(4):
                if g == 0:
                    core.claim(pe, 4)
                last = nc.tensor.transpose(bank[4][:, g * P:(g + 1) * P], sg[:, g, :], core.ident[:])
            last.then_inc(*core.filled[4].up())
            for first, bs in ((A_V, (5, 6)), (C_V, (7, 4))):
                for t in range(TT):
                    b = bs[t]
                    core.claim(pe, b)
                    for f in range(4):
                        last = nc.tensor.transpose(bank[b][:, f * P:(f + 1) * P],
                                                   pT[:, first + f, t * P:(t + 1) * P], core.ident[:])
                    last.then_inc(*core.filled[b].up())
            for h in range(H2):
                b, o = 5 + h % 3, 64 * (h % 2)
                core.claim(pe, b)
                for t in range(TT):
                    last = nc.tensor.matmul(bank[b][:, t * SEQ:(t + 1) * SEQ],
                                            pT[o:o + 64, C_Q + h // 2, t * P:(t + 1) * P],
                                            pT[o:o + 64, C_K + h // 2, :], start=True, stop=True)
                last.then_inc(*core.filled[b].up())
            pe.wait_ge(*S["av_ready"].next(pe, TT))
            for g in range(4):
                b = 4 + g // 2
                if g % 2 == 0:
                    core.claim(pe, b)
                for t in range(TT):
                    o = (g % 2) * SEQ + t * P
                    last = nc.tensor.matmul(bank[b][:, o:o + P], av[:, t, g * P:(g + 1) * P], wmT[:, g, :],
                                            start=True, stop=True)
                if g % 2:
                    last.then_inc(*core.filled[b].up())
            pe.wait_ge(*S["conv"].next(pe, 4))
            core.claim(pe, 6)
            for j in range(4):
                last = nc.tensor.matmul(bank[6][:, 0:SEQ], core.ones[:], tiles(B_GLU)[:, j, :],
                                        start=j == 0, stop=j == 3)
            last.then_inc(*core.filled[6].up())
            project(3)
            pe.wait_ge(*S["squared"].next(pe))
            core.claim(pe, 6)
            for j in range(4):
                last = nc.tensor.matmul(bank[6][:, 0:SEQ], core.ones[:], glu[:, j, 0:SEQ],
                                        start=j == 0, stop=j == 3)
            last.then_inc(*core.filled[6].up())
            for h in range(H2):
                b = h % 2
                pe.wait_ge(*S["prob_ready"].next(pe, TT))
                core.claim(pe, b)
                for c in range(TT):
                    for t in range(TT):
                        last = nc.tensor.transpose(bank[b][:, c * SEQ + t * P:c * SEQ + (t + 1) * P],
                                                   logit[:, h, t, c * P:(c + 1) * P], core.ident[:])
                last.then_inc(*core.filled[b].up())
                if h >= 1:
                    values(h - 1)
            values(H2 - 1)
            pe.wait_ge(*branch_in.next(pe))
            for n in (0, 1, 2):
                if n == 0:
                    pe.wait_ge(*S["z_ready"].next(pe))
                if n == 1:
                    pe.wait_ge(*S["yb_ready"].next(pe))
                if n == 2:
                    core.copied(pe, 2, 3)
                for q in range(4):
                    b = 4 + q
                    core.claim(pe, b)
                    for f in (2 * q, 2 * q + 1):
                        for k in range(4):
                            last = nc.tensor.matmul(bank[b][:, (f % 2) * SEQ:(f % 2 + 1) * SEQ],
                                                    wb[:, n, k, f * P:(f + 1) * P], yT[n][:, k, :],
                                                    start=k == 0, stop=k == 3)
                    last.then_inc(*core.filled[b].up())
            pe.wait_ge(*S["mixed"].next(pe, 4))
            pe.wait_ge(*out_in.next(pe, 2))
            for t in range(TT):
                for n in range(2):
                    b = 2 * t + n
                    core.claim(pe, b)
                    for k in range(KT):
                        last = nc.tensor.matmul(bank[b][:], mixedT[:, k, t * P:(t + 1) * P],
                                                w_out[k // 4][:, k % 4, n * 512:(n + 1) * 512],
                                                start=k == 0, stop=k == KT - 1)
                    last.then_inc(*core.filled[b].up())

        @block.gpsimd
        def _(pool):
            nc.gpsimd.memset(glu[:, :, 0:CONV - 1], 0.0).then_inc(*S["padded"].up())

        @block.scalar
        def _(act):
            bank, run = core.bank, nc.scalar.activation
            norm.scalar(act)
            for b in (0, 1):
                core.filled[b].passed(act, 1)

            def take(first, count, func):
                with turns(act, count, *[(core.filled[b], 1) for b in range(4)],
                           *[(core.emptied[b], 1) for b in range(4)]) as i:
                    for b in range(4):
                        act.wait_ge(*core.filled[b].next(act))
                        run(pT[:, bass.ds(i * 8 + (first + 2 * b), 2), :],
                            bank[b][:].rearrange("p (f n) -> p f n", f=2), func).then_inc(*core.emptied[b].up())
                for b in range(4):
                    act.wait_ge(*core.read(act, b))

            take(0, 3, ACT.Copy)
            run(flat(B_GLU), flat(B_GLU), ACT.Sigmoid).then_inc(*S["sig_glu"].up())
            run(flat(A_G), flat(A_G), ACT.Silu).then_inc(*S["silu_a"].up())
            run(flat(B_G), flat(B_G), ACT.Silu).then_inc(*S["silu_b"].up())
            take(24, 2, ACT.Copy)
            run(flat(C_G), flat(C_G), ACT.Silu).then_inc(*S["silu_c"].up())
            for t in range(TT):
                act.wait_ge(*S["var"].next(act))
                run(aggr[:, t, 3:4], aggr[:, t, 2:3], ACT.Sqrt).then_inc(*S["dev"].up())
            for h in range(H2):
                act.wait_ge(*S["neg_top"].next(act))
                for t in range(TT):
                    i = TT * h + t
                    run(logit[:, h, t, :], logit[:, h, t, :], ACT.Exp, bias=soft[:, 1, i:i + 1],
                        accum_out=soft[:, 2, i:i + 1]).then_inc(*S["exped"].up())
            take(MERGE, 3, ACT.Sigmoid)
            act.wait_ge(*S["centred"].next(act, 4))
            run(glu[:, :, 0:SEQ], tiles(B_GLU), ACT.Square).then_inc(*S["squared"].up())
            act.wait_ge(*S["chan_var"].next(act))
            run(chan[:, 0, :], chan[:, 1, :], ACT.Sqrt).then_inc(*S["chan_dev"].up())
            for j in range(4):
                act.wait_ge(*S["scaled"].next(act))
                run(tiles(B_GLU)[:, j, :], tiles(B_GLU)[:, j, :], ACT.Silu, scale=core.column("cv_ln_g_2", j),
                    bias=core.column("cv_ln_b_2", j)).then_inc(*S["cv_ready"].up())
            for h in range(H2):
                b = h % 2
                act.wait_ge(*core.filled[b].next(act))
                if h >= 2:
                    act.wait_ge(*core.filled[2 + b].ahead(9 + h // 2))
                run(probT[b][:], bank[b][:].rearrange("p (c n) -> p c n", c=TT), ACT.Copy)\
                    .then_inc(*core.emptied[b].up())
            for t in range(TT):
                act.wait_ge(*S["out_var"].next(act))
                run(aggr[:, t, 3:4], aggr[:, t, 2:3], ACT.Sqrt).then_inc(*S["out_dev"].up())

        @block.vector
        def _(dve):
            bank, vec, step = core.bank, nc.vector, S["step"]

            def then(op, signal=step):
                op.then_inc(*signal.up())
                dve.wait_ge(*signal.own())

            def deviation(t, stats, var, dev):
                then(vec.bn_aggr(aggr[:, t, 0:2], stats))
                vec.tensor_scalar(aggr[:, t, 2:3], aggr[:, t, 1:2], 1.0, LN_EPS, ALU.mult, ALU.add)\
                    .then_inc(*var.up())
                dve.wait_ge(*dev.next(dve))
                then(vec.reciprocal(aggr[:, t, 4:5], aggr[:, t, 3:4]))

            norm.vector(dve)
            dve.wait_ge(*S["padded"].next(dve))
            dve.wait_ge(*S["sig_glu"].next(dve))
            then(vec.tensor_tensor(glu[:, :, CONV - 1:], tiles(B_VAL), tiles(B_GLU), ALU.mult))
            for k in range(CONV):
                for j in range(4):
                    src, dst, w = glu[:, j, k:k + SEQ], tiles(B_GLU)[:, j, :], core.column("conv_w_2", 4 * k + j)
                    if k == 0:
                        op = vec.tensor_scalar(dst, src, w, core.column("conv_b_2", j), ALU.mult, ALU.add)
                    else:
                        dve.wait_ge(*step.own(3 - (j if k == CONV - 1 else 0)))
                        op = vec.scalar_tensor_tensor(dst, src, w, dst, ALU.mult, ALU.add)
                    op.then_inc(*(S["conv"] if k == CONV - 1 else step).up())
            dve.wait_ge(*consts_in.next(dve, 6))
            dve.wait_ge(*core.filled[4].next(dve))
            for g in range(4):
                op = vec.tensor_tensor(wmT[:, g, :], bank[4][:, g * P:(g + 1) * P], upper[:], ALU.mult)
            op.then_inc(*core.emptied[4].up())
            for b in (5, 6):
                dve.wait_ge(*core.filled[b].next(dve))
            for t in range(TT):
                then(vec.bn_stats(stat[:, t, 0, :], bank[5 + t][:]))
                deviation(t, stat[:, t, 0:1, :], S["var"], S["dev"])
                vec.tensor_scalar(tmp[:], bank[5 + t][:], aggr[:, t, 0:1], aggr[:, t, 4:5], ALU.subtract, ALU.mult)\
                    .then_inc(*core.emptied[5 + t].up())
                dve.wait_ge(*core.read(dve, 5 + t))
                then(vec.tensor_tensor(tmp[:], tmp[:], rows[:, 0, :], ALU.mult))
                vec.tensor_tensor(av[:, t, :], tmp[:], rows[:, 1, :], ALU.add).then_inc(*S["av_ready"].up())
                dve.wait_ge(*S["av_ready"].own())
            for b in (7, 4):
                dve.wait_ge(*core.filled[b].next(dve))
            for t, b in enumerate((7, 4)):
                vec.tensor_copy(vtok[:, t, :], bank[b][:]).then_inc(*core.emptied[b].up())
            for h in range(H2):
                b = 5 + h % 3
                then(vec.tensor_scalar(tmp[:], dist[:], -slopes[h], None, ALU.mult))
                dve.wait_ge(*core.filled[b].next(dve))
                vec.scalar_tensor_tensor(logit[:, h, :, :].rearrange("p t n -> p (t n)"), bank[b][:], SC, tmp[:],
                                         ALU.mult, ALU.add).then_inc(*core.emptied[b].up())
                dve.wait_ge(*core.read(dve, b))
                then(vec.reduce_max(soft[:, 0, TT * h:TT * h + TT], logit[:, h, :, :], AX))
                vec.tensor_scalar(soft[:, 1, TT * h:TT * h + TT], soft[:, 0, TT * h:TT * h + TT], -1.0, None,
                                  ALU.mult).then_inc(*S["neg_top"].up())
            dve.wait_ge(*S["silu_a"].next(dve))
            for g in range(4):
                b = 4 + g // 2
                if g % 2 == 0:
                    dve.wait_ge(*core.filled[b].next(dve))
                if g == 0:
                    dve.wait_ge(*core.filled[5].ahead(5))
                for t in range(TT):
                    o = (g % 2) * SEQ + t * P
                    op = vec.tensor_tensor(tiles(A_V)[:, g, t * P:(t + 1) * P], bank[b][:, o:o + P],
                                           rows[:, 2, g * P:(g + 1) * P], ALU.add)
                    if g % 2 and t == TT - 1:
                        op.then_inc(*core.emptied[b].up())
            dve.wait_ge(*core.read(dve, 5))
            then(vec.tensor_tensor(tiles(A_U), tiles(A_U), tiles(A_V), ALU.mult))
            vec.tensor_tensor(tiles(A_U), tiles(A_U), tiles(A_G), ALU.mult).then_inc(*S["z_ready"].up())
            dve.wait_ge(*core.filled[6].next(dve))
            vec.tensor_scalar(chan[:, 0, :], bank[6][:, 0:SEQ], 1.0 / D_A, None, ALU.mult)\
                .then_inc(*core.emptied[6].up())
            dve.wait_ge(*core.read(dve, 6))
            for j in range(4):
                vec.tensor_tensor(tiles(B_GLU)[:, j, :], tiles(B_GLU)[:, j, :], chan[:, 0, :], ALU.subtract)\
                    .then_inc(*S["centred"].up())
            for h in range(H2):
                for t in range(TT):
                    i = TT * h + t
                    dve.wait_ge(*S["exped"].next(dve))
                    then(vec.reciprocal(soft[:, 3, i:i + 1], soft[:, 2, i:i + 1]))
                    vec.tensor_scalar(logit[:, h, t, :], logit[:, h, t, :], soft[:, 3, i:i + 1], None, ALU.mult)\
                        .then_inc(*S["prob_ready"].up())
            dve.wait_ge(*core.filled[6].next(dve))
            dve.wait_ge(*S["centred"].own())
            vec.tensor_scalar(chan[:, 1, :], bank[6][:, 0:SEQ], 1.0 / D_A, LN_EPS, ALU.mult, ALU.add)\
                .then_inc(*core.emptied[6].up())
            dve.wait_ge(*core.read(dve, 6))
            vec.tensor_copy(soft[:, 0, 0:1], soft[:, 1, 0:1]).then_inc(*S["chan_var"].up())
            dve.wait_ge(*S["chan_dev"].next(dve))
            then(vec.reciprocal(chan[:, 1, :], chan[:, 0, :]))
            for j in range(4):
                vec.tensor_tensor(tiles(B_GLU)[:, j, :], tiles(B_GLU)[:, j, :], chan[:, 1, :], ALU.mult)\
                    .then_inc(*S["scaled"].up())
            dve.wait_ge(*S["cv_ready"].next(dve, 4))
            dve.wait_ge(*S["silu_b"].next(dve))
            vec.tensor_tensor(tiles(B_VAL), tiles(B_GLU), tiles(B_G), ALU.mult).then_inc(*S["yb_ready"].up())
            dve.wait_ge(*S["silu_c"].next(dve))
            for b in (2, 3):
                core.filled[b].passed(dve, 9)
            for h in range(H2):
                b, o = 2 + h % 2, 64 * (h % 2)
                dve.wait_ge(*core.filled[b].next(dve))
                vec.tensor_tensor(tiles(C_Q)[o:o + 64, h // 2, :], bank[b][o:o + 64, 0:SEQ],
                                  tiles(C_G)[o:o + 64, h // 2, :], ALU.mult).then_inc(*core.emptied[b].up())
            for b in range(4):
                dve.wait_ge(*core.emptied[b].ahead(9))
            for n in range(3):
                for q in range(4):
                    b = 4 + q
                    gate, mixed = tiles(MERGE + 8 * n + 2 * q, 2), mixedT[:, 2 * q:2 * q + 2, :]
                    src = bank[b][:].rearrange("p (f n) -> p f n", f=2)
                    dve.wait_ge(*core.filled[b].next(dve))
                    if n == 0:
                        vec.tensor_tensor(mixed, src, gate, ALU.mult).then_inc(*core.emptied[b].up())
                        dve.wait_ge(*core.read(dve, b))
                    else:
                        vec.tensor_tensor(gate, src, gate, ALU.mult).then_inc(*core.emptied[b].up())
                        dve.wait_ge(*core.read(dve, b))
                        vec.tensor_tensor(mixed, mixed, gate, ALU.add)\
                            .then_inc(*(S["mixed"] if n == 2 else step).up())
                        dve.wait_ge(*(S["mixed"] if n == 2 else step).own())
            for b in (0, 1):
                core.filled[b].passed(dve, 12)
            for t in range(TT):
                for n in range(2):
                    b, o = 2 * t + n, slice(n * 512, (n + 1) * 512)
                    dve.wait_ge(*core.filled[b].next(dve))
                    vec.scalar_tensor_tensor(core.x[:, t, o], core.x[:, t, o], ALPHA, bank[b][:], ALU.mult, ALU.add)\
                        .then_inc(*core.emptied[b].up())
                    dve.wait_ge(*core.read(dve, b))
                    then(vec.bn_stats(stat[:, t, n, :], core.x[:, t, o]))
                deviation(t, stat[:, t, :, :], S["out_var"], S["out_dev"])
                then(vec.tensor_scalar(core.x[:, t, :], core.x[:, t, :], aggr[:, t, 0:1], aggr[:, t, 4:5],
                                       ALU.subtract, ALU.mult))
                if t == 0:
                    dve.wait_ge(*ln_in.next(dve, 2))
                then(vec.tensor_tensor(core.x[:, t, :], core.x[:, t, :], ln_rows[:, 0, :], ALU.mult))
                then(vec.tensor_tensor(core.x[:, t, :], core.x[:, t, :], ln_rows[:, 1, :], ALU.add))



def ffn(core, layer, which, scale, shift, gate):
    nc, ins = core.nc, core.ins
    F = 256
    steps = DFF3 // F
    with Stage(core, f"ffn{layer}{which}") as st:
        wgu = st.sb("wgu", [P, 2, 2, KT, F])
        wd = st.sb("wd", [P, 2, 2, D])
        actT = st.sb("actT", [P, 2, 2, SEQ])
        silu = st.sb("silu", [P, 4, SEQ])
        norm = Norm(st, core.x, core.hT, scale, shift)
        gu_in = [st.landed(f"gu_in{s}") for s in range(2)]
        wd_in = [st.landed(f"wd_in{s}") for s in range(2)]
        wd_used, silu_ready, step = st.sem("wd_used"), st.sem("silu_ready"), st.sem("step")
        block = st.block()
        w_gu = ins["ffn_w_gu_3"][layer, which].rearrange("(k p) n -> p k n", p=P)
        w_down = ins["ffn_w_down_3"][layer, which]

        @block.sync
        def _(sp):
            def load_gu(s, at):
                sp.dma_start(wgu[:, s, 0], w_gu[:, :, at(0)]).then_inc(*gu_in[s].up())
                sp.dma_start(wgu[:, s, 1], w_gu[:, :, at(DFF3)]).then_inc(*gu_in[s].up())

            def load_wd(s, at):
                sp.dma_start(wd[:, s], w_down[at(0), :].rearrange("(f p) n -> p f n", p=P)).then_inc(*wd_in[s].up())

            for s in range(2):
                load_gu(s, lambda o: slice(o + s * F, o + (s + 1) * F))
                load_wd(s, lambda o: slice(o + s * F, o + (s + 1) * F))
            with turns(sp, (steps - 3) // 2, *[(x, 2) for x in gu_in], *[(x, 1) for x in wd_in],
                       (core.filled[5], 1), (core.filled[7], 1), (wd_used, 2)) as i:
                for s in range(2):
                    at = lambda o: bass.ds(i * (2 * F) + (2 * F + s * F + o), F)
                    sp.wait_ge(*core.filled[5 + 2 * s].next(sp))
                    load_gu(s, at)
                    sp.wait_ge(*wd_used.next(sp))
                    load_wd(s, at)
            sp.wait_ge(*core.filled[5].next(sp))
            load_gu(0, lambda o: slice(o + DFF3 - F, o + DFF3))
            sp.wait_ge(*wd_used.next(sp))
            load_wd(0, lambda o: slice(o + DFF3 - F, o + DFF3))

        @block.tensor
        def _(pe):
            bank = core.bank
            norm.tensor(pe)

            def up(s):
                pe.wait_ge(*gu_in[s].next(pe, 2))
                for f in range(2):
                    b = 4 + 2 * s + f
                    core.claim(pe, b)
                    for m in range(2):
                        for k in range(KT):
                            last = nc.tensor.matmul(bank[b][:, m * SEQ:(m + 1) * SEQ],
                                                    wgu[:, s, m, k, f * P:(f + 1) * P], core.hT[:, k, :],
                                                    start=k == 0, stop=k == KT - 1)
                    last.then_inc(*core.filled[b].up())

            def down(s, start=False, stop=False):
                pe.wait_ge(*wd_in[s].next(pe))
                core.copied(pe, 4 + 2 * s, 5 + 2 * s)
                for t in range(TT):
                    for n in range(2):
                        b = 2 * t + n
                        if start:
                            core.claim(pe, b)
                        for f in range(2):
                            last = nc.tensor.matmul(bank[b][:], actT[:, s, f, t * P:(t + 1) * P],
                                                    wd[:, s, f, n * 512:(n + 1) * 512],
                                                    start=start and f == 0, stop=stop and f == 1)
                        if stop:
                            last.then_inc(*core.filled[b].up())
                if not stop:
                    last.then_inc(*wd_used.up())

            up(0)
            up(1)
            down(0, start=True)
            with turns(pe, (steps - 3) // 2, *[(x, 2) for x in gu_in], *[(x, 1) for x in wd_in],
                       *[(core.filled[b], 1) for b in range(4, 8)], (wd_used, 2)):
                up(0)
                down(1)
                up(1)
                down(0)
            up(0)
            down(1)
            down(0, stop=True)

        @block.scalar
        def _(act):
            norm.scalar(act)

            def silus(s):
                for b in (4 + 2 * s, 5 + 2 * s):
                    act.wait_ge(*core.filled[b].next(act))
                    nc.scalar.activation(silu[:, b - 4, :], core.bank[b][:, 0:SEQ], ACT.Silu)\
                        .then_inc(*silu_ready.up())

            silus(0)
            silus(1)
            with turns(act, (steps - 3) // 2, *[(core.filled[b], 1) for b in range(4, 8)], (silu_ready, 4)):
                silus(0)
                silus(1)
            silus(0)

        @block.vector
        def _(dve):
            vec = nc.vector
            norm.vector(dve)

            def products(s):
                for f in range(2):
                    b = 4 + 2 * s + f
                    dve.wait_ge(*silu_ready.next(dve))
                    vec.tensor_tensor(actT[:, s, f, :], silu[:, b - 4, :], core.bank[b][:, SEQ:], ALU.mult)\
                        .then_inc(*core.emptied[b].up())

            products(0)
            products(1)
            with turns(dve, (steps - 3) // 2, *[(core.emptied[b], 1) for b in range(4, 8)], (silu_ready, 4)):
                products(0)
                products(1)
            products(0)
            for b in (2, 3):
                core.filled[b].passed(dve, 1)
            residual(core, dve, gate, norm.xn, step)


def residual(core, dve, gate, junk, step):
    vec = core.nc.vector
    for t in range(TT):
        for n in range(2):
            b, o = 2 * t + n, slice(n * 512, (n + 1) * 512)
            dve.wait_ge(*core.filled[b].next(dve))
            vec.tensor_tensor(junk[:, t, o], core.bank[b][:], gate[:, o], ALU.mult).then_inc(*core.emptied[b].up())
            dve.wait_ge(*core.read(dve, b))
            vec.tensor_tensor(core.x[:, t, o], core.x[:, t, o], junk[:, t, o], ALU.add).then_inc(*step.up())


def pool_mixer(core, scale, shift, gate):
    nc, ins = core.nc, core.ins
    EDGE, L = 8, SEQ + 16
    with Stage(core, "pool") as st:
        hp, sa, sb_ = [st.sb(n, [P, KT, L]) for n in ("padded", "sums_a", "sums_b")]
        dT = core.hT
        pw = st.sb("pw", [P, 4, 2, 256])
        inv = st.sb("inv", [P, 4, SEQ])
        norm = Norm(st, core.x, hp[:, :, EDGE:EDGE + SEQ], scale, shift)
        w_in, inv_in = st.landed("w_in"), st.landed("inv_in")
        edges, diff, step = st.sem("edges"), st.sem("diff"), st.sem("step")
        block = st.block()

        @block.sync
        def _(sp):
            sp.dma_start(pw[:], ins["pool_w_3"].rearrange("g (k p) n -> p g k n", p=P)).then_inc(*w_in.up())
            sp.dma_start(inv[:], core.ins["tables"][:, AT["count"]:AT["count"] + 1024]
                         .rearrange("p (g n) -> p g n", g=4)).then_inc(*inv_in.up())

        @block.gpsimd
        def _(pool):
            nc.gpsimd.memset(hp[:, :, 0:EDGE], 0.0).then_inc(*edges.up())
            nc.gpsimd.memset(hp[:, :, L - EDGE:L], 0.0).then_inc(*edges.up())

        @block.scalar
        def _(act):
            norm.scalar(act)

        @block.tensor
        def _(pe):
            norm.tensor(pe)
            pe.wait_ge(*w_in.next(pe))
            pe.wait_ge(*diff.next(pe, 4))
            for t in range(TT):
                for n in range(2):
                    b = 2 * t + n
                    core.claim(pe, b)
                    for g in (2 * n, 2 * n + 1):
                        for k in range(2):
                            last = nc.tensor.matmul(core.bank[b][:, (g % 2) * 256:(g % 2 + 1) * 256],
                                                    dT[:, 2 * g + k, t * P:(t + 1) * P], pw[:, g, k, :],
                                                    start=k == 0, stop=k == 1)
                    last.then_inc(*core.filled[b].up())

        @block.vector
        def _(dve):
            vec = nc.vector
            norm.vector(dve)
            for b in (0, 1):
                dve.wait_ge(*core.read(dve, b))
            for b in (2, 3):
                dve.wait_ge(*core.emptied[b].next(dve))
            dve.wait_ge(*edges.next(dve, 2))
            dve.wait_ge(*inv_in.next(dve))
            sums = [hp, sa, sb_, sa, sb_]
            for g in range(4):
                half = 1 if g == 0 else 1 << (g - 1)
                lo, a = 1 << g, 2 * g
                if g == 0:
                    left, right = hp[:, :, 0:L - 1], hp[:, :, 1:L]
                    out = sa[:, :, 1:L]
                else:
                    left = sums[g][:, a:, lo - half:L - lo - half]
                    right = sums[g][:, a:, lo + half:L - lo + half]
                    out = sums[g + 1][:, a:, lo:L - lo]
                vec.tensor_tensor(out, left, right, ALU.add).then_inc(*step.up())
                dve.wait_ge(*step.own())
                for j in (a, a + 1):
                    vec.tensor_tensor(dT[:, j, :], sums[g + 1][:, j, EDGE:EDGE + SEQ], inv[:, g, :], ALU.mult)\
                        .then_inc(*step.up())
                dve.wait_ge(*step.own())
                vec.tensor_tensor(dT[:, a:a + 2, :], dT[:, a:a + 2, :], hp[:, a:a + 2, EDGE:EDGE + SEQ],
                                  ALU.subtract).then_inc(*diff.up())
            for b in (2, 3):
                core.filled[b].passed(dve, 1)
            residual(core, dve, gate, norm.xn, step)


def diff_attention(core, scale, shift, gate):
    nc, ins = core.nc, core.ins
    SC = DH3 ** -0.5
    with Stage(core, "diff") as st:
        wqk = st.sb("wqk", [P, KT, 2 * D])
        wv = st.sb("wv", [P, KT, D])
        w_o = wqk[:, 0:4, :].rearrange("p a b -> p (a b)").rearrange("p (k n) -> p k n", n=D)
        qk = st.sb("qk", [P, 2 * KT, SEQ])
        v = st.sb("v", [P, TT, D])
        cs = st.sb("cs", [P, 2, SEQ])
        turn = st.sb("turn", [P, P])
        rot = st.sb("rot", [P, 2, SEQ])
        prob = [st.sb(f"prob{i}", [P, TT, 2, SEQ]) for i in range(2)]
        probT = [st.sb(f"probT{i}", [P, TT, SEQ]) for i in range(2)]
        lamrow = st.sb("lamrow", [P, 4, DH3])
        lam = st.sb("lam", [P, 8])
        soft = st.sb("soft", [P, 4, H3 * TT * 2])
        ostat = st.sb("ostat", [P, 4, TT * H3])
        subln = st.sb("subln", [P, 1])
        norm = Norm(st, core.x, core.hT, scale, shift)
        o = norm.xn
        oT = core.hT
        qk_in, v_in, o_in, small_in = [st.landed(n) for n in ("qk_in", "v_in", "o_in", "small_in")]
        S = {n: st.sem(n) for n in ("turned", "lam_sum", "lam_exp", "neg_top", "mixed", "prob_ready", "o_sq",
                                       "o_mean", "o_root", "o_ready", "step", "exped")}
        block = st.block()
        w = ins["diff_w_qkv_3"].rearrange("(k p) n -> p k n", p=P)

        @block.sync
        def _(sp):
            sp.dma_start(wqk[:], w[:, :, 0:2 * D]).then_inc(*qk_in.up())
            for i, name in enumerate(("cos3", "sin3")):
                sp.dma_start(cs[:, i, :], ins["tables"][:, AT[name]:AT[name] + SEQ]).then_inc(*small_in.up())
            sp.dma_start(turn[:], ins["tables"][:, AT["turn3"]:AT["turn3"] + P]).then_inc(*small_in.up())
            sp.dma_start(lamrow[:].rearrange("p a b -> p (a b)"), ins["diff_lambda_3"].partition_broadcast(P))\
                .then_inc(*small_in.up())
            sp.dma_start(wv[:], w[:, :, 2 * D:]).then_inc(*v_in.up())
            sp.wait_ge(*core.filled[6].ahead(1))
            sp.dma_start(w_o, ins["diff_w_o_3"].rearrange("(k p) n -> p k n", p=P)).then_inc(*o_in.up())

        @block.tensor
        def _(pe):
            bank = core.bank
            norm.tensor(pe)
            pe.wait_ge(*qk_in.next(pe))
            pe.wait_ge(*small_in.next(pe, 4))

            def turned(q):
                core.copied(pe, q % 4)
                b = 4 + q % 2
                core.claim(pe, b)
                for f in range(2):
                    last = nc.tensor.matmul(bank[b][:, f * SEQ:(f + 1) * SEQ], turn[:], qk[:, 2 * q + f, :],
                                            start=True, stop=True)
                last.then_inc(*core.filled[b].up())

            for q in range(KT):
                core.claim(pe, q % 4)
                for f in range(2):
                    for k in range(KT):
                        a = (2 * q + f) * P
                        last = nc.tensor.matmul(bank[q % 4][:, f * SEQ:(f + 1) * SEQ], wqk[:, k, a:a + P],
                                                core.hT[:, k, :], start=k == 0, stop=k == KT - 1)
                last.then_inc(*core.filled[q % 4].up())
                if q:
                    turned(q - 1)
            turned(KT - 1)
            pe.wait_ge(*v_in.next(pe))
            for t in range(TT):
                for n in range(2):
                    core.claim(pe, 6 + n)
                    for k in range(KT):
                        last = nc.tensor.matmul(bank[6 + n][:], core.hT[:, k, t * P:(t + 1) * P],
                                                wv[:, k, n * 512:(n + 1) * 512], start=k == 0, stop=k == KT - 1)
                    last.then_inc(*core.filled[6 + n].up())

            def scores(h):
                for c in range(2):
                    b = 2 * (h % 2) + c
                    core.claim(pe, b)
                    for t in range(TT):
                        last = nc.tensor.matmul(bank[b][:, t * SEQ:(t + 1) * SEQ],
                                                qk[64 * c:64 * c + 64, h, t * P:(t + 1) * P],
                                                qk[64 * c:64 * c + 64, KT + h, :], start=True, stop=True)
                    last.then_inc(*core.filled[b].up())

            def attend(h):
                b = 4 + h % 2
                pe.wait_ge(*S["prob_ready"].next(pe, TT))
                core.claim(pe, b)
                for c in range(TT):
                    for t in range(TT):
                        last = nc.tensor.transpose(bank[b][:, c * SEQ + t * P:c * SEQ + (t + 1) * P],
                                                   prob[h % 2][:, t, 0, c * P:(c + 1) * P], core.ident[:])
                last.then_inc(*core.filled[b].up())
                core.copied(pe, b)
                b = 6 + h % 2
                core.claim(pe, b)
                for t in range(TT):
                    for c in range(TT):
                        last = nc.tensor.matmul(bank[b][:, t * P:(t + 1) * P], probT[h % 2][:, c, t * P:(t + 1) * P],
                                                v[:, c, h * P:(h + 1) * P], start=c == 0, stop=c == TT - 1)
                last.then_inc(*core.filled[b].up())

            pe.wait_ge(*S["turned"].next(pe, KT))
            core.copied(pe, 6, 7)
            scores(0)
            for h in range(H3):
                if h + 1 < H3:
                    scores(h + 1)
                attend(h)
            pe.wait_ge(*S["o_ready"].next(pe))
            for q in range(4):
                core.claim(pe, q)
                for f in range(2):
                    for t in range(TT):
                        a = (2 * q + f) * P
                        last = nc.tensor.transpose(bank[q][:, f * SEQ + t * P:f * SEQ + (t + 1) * P],
                                                   o[:, t, a:a + P], core.ident[:])
                last.then_inc(*core.filled[q].up())
            core.copied(pe, 0, 1, 2, 3)
            pe.wait_ge(*o_in.next(pe))
            for t in range(TT):
                for n in range(2):
                    b = 2 * t + n
                    core.claim(pe, b)
                    for k in range(KT):
                        last = nc.tensor.matmul(bank[b][:], oT[:, k, t * P:(t + 1) * P],
                                                w_o[:, k, n * 512:(n + 1) * 512], start=k == 0, stop=k == KT - 1)
                    last.then_inc(*core.filled[b].up())

        @block.scalar
        def _(act):
            bank, run = core.bank, nc.scalar.activation
            norm.scalar(act)
            for b in (0, 1):
                core.filled[b].passed(act, 1)
            for q in range(KT):
                act.wait_ge(*core.filled[q % 4].next(act))
                run(qk[:, 2 * q:2 * q + 2, :], bank[q % 4][:].rearrange("p (f n) -> p f n", f=2), ACT.Copy)\
                    .then_inc(*core.emptied[q % 4].up())
            for t in range(TT):
                for n in range(2):
                    act.wait_ge(*core.filled[6 + n].next(act))
                    run(v[:, t, n * 512:(n + 1) * 512], bank[6 + n][:], ACT.Copy).then_inc(*core.emptied[6 + n].up())
            act.wait_ge(*S["lam_sum"].next(act))
            run(lam[:, 2:4], lam[:, 0:2], ACT.Exp).then_inc(*S["lam_exp"].up())

            def exponents(h):
                act.wait_ge(*S["neg_top"].next(act))
                for c in range(2):
                    b = 2 * (h % 2) + c
                    for t in range(TT):
                        i = (h * 2 + c) * TT + t
                        run(prob[h % 2][:, t, c, :], bank[b][:, t * SEQ:(t + 1) * SEQ], ACT.Exp,
                            bias=soft[:, 1, i:i + 1], scale=SC, accum_out=soft[:, 2, i:i + 1])\
                            .then_inc(*(S["exped"] if t == 0 else core.emptied[b]).up())

            def transposed(h):
                b = 4 + h % 2
                act.wait_ge(*core.filled[b].next(act))
                run(probT[h % 2][:], bank[b][:].rearrange("p (c n) -> p c n", c=TT), ACT.Copy)\
                    .then_inc(*core.emptied[b].up())

            for b in (4, 5):
                core.filled[b].passed(act, 4)
            exponents(0)
            for h in range(H3):
                if h + 1 < H3:
                    exponents(h + 1)
                transposed(h)
            act.wait_ge(*S["mixed"].next(act))
            run(wv[:, 0:2, :], o[:], ACT.Square).then_inc(*S["o_sq"].up())
            act.wait_ge(*S["o_mean"].next(act))
            run(ostat[:, 2, :], ostat[:, 1, :], ACT.Sqrt).then_inc(*S["o_root"].up())

        @block.vector
        def _(dve):
            bank, vec, step = core.bank, nc.vector, S["step"]

            def then(op, signal=step):
                op.then_inc(*signal.up())
                dve.wait_ge(*signal.own())

            norm.vector(dve)
            dve.wait_ge(*small_in.next(dve, 4))
            for i in range(2):
                then(vec.tensor_tensor(rot[:, i, 0:DH3], lamrow[:, 2 * i, :], lamrow[:, 2 * i + 1, :], ALU.mult))
            then(vec.reduce_sum(lam[:, 0:2], rot[:, :, 0:DH3], AX), S["lam_sum"])
            for q in range(KT):
                b = 4 + q % 2
                dve.wait_ge(*core.filled[b].next(dve))
                for f in range(2):
                    op = vec.tensor_tensor(rot[:, f, :], bank[b][:, f * SEQ:(f + 1) * SEQ], cs[:, 1, :], ALU.mult)
                op.then_inc(*core.emptied[b].up())
                for f in range(2):
                    vec.tensor_tensor(qk[:, 2 * q + f, :], qk[:, 2 * q + f, :], cs[:, 0, :], ALU.mult)\
                        .then_inc(*step.up())
                dve.wait_ge(*step.own())
                then(vec.tensor_tensor(qk[:, 2 * q:2 * q + 2, :], qk[:, 2 * q:2 * q + 2, :], rot[:], ALU.add),
                     S["turned"])
            dve.wait_ge(*S["lam_exp"].next(dve))
            then(vec.tensor_tensor(lam[:, 4:5], lam[:, 3:4], lam[:, 2:3], ALU.subtract))
            then(vec.tensor_scalar(lam[:, 5:6], lam[:, 4:5], LAM_INIT, None, ALU.subtract))
            then(vec.tensor_scalar(subln[:], core.column("diff_subln_g_3"), 1.0 - LAM_INIT, None, ALU.mult))
            for b in (0, 1):
                core.filled[b].passed(dve, 2)
            for b in (2, 3):
                core.filled[b].passed(dve, 3)
            for b in (6, 7):
                core.filled[b].passed(dve, 2)
            for b in range(4):
                core.emptied[b].passed(dve, 3)

            def maxima(h):
                for c in range(2):
                    b, i = 2 * (h % 2) + c, (h * 2 + c) * TT
                    dve.wait_ge(*core.filled[b].next(dve))
                    then(vec.reduce_max(soft[:, 0, i:i + 2], bank[b][:].rearrange("p (t n) -> p t n", t=TT), AX))
                i = h * TT * 2
                vec.tensor_scalar(soft[:, 1, i:i + 4], soft[:, 0, i:i + 4], -SC, None, ALU.mult)\
                    .then_inc(*S["neg_top"].up())

            def finish(h):
                p = prob[h % 2]
                for c in range(2):
                    dve.wait_ge(*core.emptied[2 * (h % 2) + c].next(dve))
                then(vec.reciprocal(soft[:, 3, 4 * h:4 * h + 4], soft[:, 2, 4 * h:4 * h + 4]))
                for t in range(TT):
                    i = 4 * h + t
                    then(vec.tensor_scalar(p[:, t, 1, :], p[:, t, 1, :], soft[:, 3, i + 2:i + 3], lam[:, 5:6],
                                           ALU.mult, ALU.mult))
                    vec.scalar_tensor_tensor(p[:, t, 0, :], p[:, t, 0, :], soft[:, 3, i:i + 1], p[:, t, 1, :],
                                             ALU.mult, ALU.add).then_inc(*S["prob_ready"].up())
                b = 6 + h % 2
                dve.wait_ge(*core.filled[b].next(dve))
                vec.tensor_copy(o[:, :, h * P:(h + 1) * P], bank[b][:, 0:SEQ].rearrange("p (t n) -> p t n", t=TT))\
                    .then_inc(*core.emptied[b].up())

            maxima(0)
            for h in range(H3):
                if h + 1 < H3:
                    maxima(h + 1)
                finish(h)
            dve.wait_ge(*core.read(dve, 6))
            dve.wait_ge(*core.read(dve, 7))
            vec.tensor_copy(lam[:, 6:7], lam[:, 5:6]).then_inc(*S["mixed"].up())
            dve.wait_ge(*S["o_sq"].next(dve))
            heads = lambda a: a.rearrange("p t (h n) -> p t h n", h=H3)
            then(vec.reduce_sum(ostat[:, 0, :].rearrange("p (t h) -> p t h", t=TT), heads(wv[:, 0:2, :]), AX))
            vec.tensor_scalar(ostat[:, 1, :], ostat[:, 0, :], 1.0 / P, RMS_EPS, ALU.mult, ALU.add)\
                .then_inc(*S["o_mean"].up())
            dve.wait_ge(*S["o_root"].next(dve))
            then(vec.reciprocal(ostat[:, 3, :], ostat[:, 2, :]))
            for t in range(TT):
                for h in range(H3):
                    i = t * H3 + h
                    op = vec.tensor_scalar(o[:, t, h * P:(h + 1) * P], o[:, t, h * P:(h + 1) * P],
                                           ostat[:, 3, i:i + 1], None, ALU.mult)
            op.then_inc(*S["o_ready"].up())
            for q in range(4):
                dve.wait_ge(*core.filled[q].next(dve))
                vec.tensor_scalar(oT[:, 2 * q:2 * q + 2, :], bank[q][:].rearrange("p (f n) -> p f n", f=2),
                                  subln[:], None, ALU.mult).then_inc(*core.emptied[q].up())
            residual(core, dve, gate, wv, step)


def final_norm(core):
    nc, ins = core.nc, core.ins
    with Stage(core, "final") as st:
        gain = st.sb("gain", [P, D])
        y = st.sb("y", [P, TT, D])
        small = st.sb("small", [P, 4 * TT])
        gain_in, stored = st.landed("gain_in"), st.landed("stored")
        sum_sq, mean_sq, root, inv, done = [st.sem(n) for n in ("sum_sq", "mean_sq", "root", "inv", "done")]
        block = st.block()

        @block.sync
        def _(sp):
            sp.dma_start(gain[:], ins["final_g_3"].partition_broadcast(P)).then_inc(*gain_in.up())
            for t in range(TT):
                sp.wait_ge(*done.next(sp))
                sp.dma_start(core.out[:, t, :], y[:, t, :]).then_inc(*stored.up())
            sp.wait_ge(*stored.next(sp, TT))

        @block.scalar
        def _(act):
            for t in range(TT):
                nc.scalar.activation(y[:, t, :], core.x[:, t, :], ACT.Square, accum_out=small[:, t:t + 1])\
                    .then_inc(*sum_sq.up())
            act.wait_ge(*mean_sq.next(act))
            nc.scalar.activation(small[:, 4:4 + TT], small[:, 2:2 + TT], ACT.Sqrt).then_inc(*root.up())

        @block.vector
        def _(dve):
            dve.wait_ge(*sum_sq.next(dve, TT))
            nc.vector.tensor_scalar(small[:, 2:2 + TT], small[:, 0:TT], 1.0 / D, RMS_EPS, ALU.mult, ALU.add)\
                .then_inc(*mean_sq.up())
            dve.wait_ge(*root.next(dve))
            nc.vector.reciprocal(small[:, 6:6 + TT], small[:, 4:4 + TT]).then_inc(*inv.up())
            dve.wait_ge(*inv.own())
            dve.wait_ge(*gain_in.next(dve))
            for t in range(TT):
                nc.vector.scalar_tensor_tensor(y[:, t, :], core.x[:, t, :], small[:, 6 + t:7 + t], gain[:],
                                               ALU.mult, ALU.mult).then_inc(*done.up())


def third(core):
    nc, ins = core.nc, core.ins
    with Stage(core, "third") as st:
        mod = st.sb("mod", [P, LAYERS, 6, KT])
        gate = st.sb("gate", [P, 3, D])
        b_mod = ins["mod_b_3_row"]
        for layer in range(LAYERS):
            at = layer * MODS3
            gain = [core.column("norm_g_3", (layer * 3 + n) * KT, KT) for n in range(3)]
            wanted = [(3 * n + m, gain[n] if m else None, mod[:, layer, 2 * n + m, :])
                      for n in range(3) for m in range(2)]
            own = [0.5, ins["pool_scale_3"] if layer == 0 else 1.0, 0.5]
            rows = [(3 * n + 2, b_mod[(at + 3 * n + 2) * D:(at + 3 * n + 3) * D], own[n], gate[:, n, :])
                    for n in range(3)]
            modulation(core, f"mod3{layer}", ins["c_3"], ins["mod_w_3"][layer], MODS3, wanted, rows,
                       lambda piece: core.column("mod_b_3", (at + piece) * KT, KT))
            ffn(core, layer, 0, mod[:, layer, 1, :], mod[:, layer, 0, :], gate[:, 0, :])
            (pool_mixer if layer == 0 else diff_attention)(core, mod[:, layer, 3, :], mod[:, layer, 2, :],
                                                           gate[:, 1, :])
            ffn(core, layer, 1, mod[:, layer, 5, :], mod[:, layer, 4, :], gate[:, 2, :])
    final_norm(core)



def store(core):
    nc = core.nc
    with Stage(core, "store") as st:
        stored = st.landed("stored")
        block = st.block()

        @block.sync
        def _(sp):
            sp.dma_start(core.out, core.x[:]).then_inc(*stored.up())
            sp.wait_ge(*stored.next(sp))


def first(core):
    nc, ins = core.nc, core.ins
    with Stage(core, "first") as st:
        core.mod1, core.gate1 = st.sb("mod1", [P, 6, KT]), st.sb("gate1", [P, 2, D])
        pre = {name: core.column(name, 0, KT) for name in ("norm_attn_pre", "norm_ffn_pre")}
        b_mod = ins["b_mod_row"]
        modulation(core, "mod1", ins["c"], ins["w_mod"], 6,
                   [(0, None, core.mod1[:, 0, :]), (1, pre["norm_attn_pre"], core.mod1[:, 1, :]),
                    (3, None, core.mod1[:, 4, :]), (4, pre["norm_ffn_pre"], core.mod1[:, 5, :])],
                   [(2, b_mod[2 * D:3 * D], 1.0, core.gate1[:, 0, :]), (5, b_mod[5 * D:6 * D], 1.0, core.gate1[:, 1, :])],
                   lambda piece: core.column("b_mod", piece * KT, KT), ins["c_ctx"],
                   [(0, None, core.mod1[:, 2, :]), (1, pre["norm_attn_pre"], core.mod1[:, 3, :])])
        mla(core)
        experts(core)


def program(nc, ins, out):
    with ExitStack() as ctx:
        core = Core(ctx, nc, ins, out)
        load_constants(core)
        first(core)
        core.clear_signals()
        second(core)
        core.clear_signals()
        third(core)


def tables():
    t = {}
    t["ident"] = np.eye(P)
    grid_w, half = 64, ROPE // 2
    n = np.arange(SEQ)
    inv = (1.0 / (np.float32(10000.0) ** (np.arange(0, half, 2, dtype=np.float32) / np.float32(half)))).astype(np.float32)
    ang = np.concatenate([(n // grid_w).astype(np.float32)[:, None] * inv, (n % grid_w).astype(np.float32)[:, None] * inv],
                         axis=-1).astype(np.float32)
    pad = lambda a: np.concatenate([a, np.zeros((P - a.shape[0], a.shape[1]))])
    t["cos1"] = pad(np.repeat(np.cos(ang.astype(np.float64)).T, 2, axis=0))
    t["sin1"] = pad(np.repeat(np.sin(ang.astype(np.float64)).T, 2, axis=0))
    turn = np.zeros((ROPE, ROPE))
    for i in range(0, ROPE, 2):
        turn[i, i + 1], turn[i + 1, i] = -1.0, 1.0
    t["turn1"] = pad(turn.T)
    a = 2 * np.pi * (np.outer(n, n) % SEQ) / SEQ
    tiled = lambda m: m.reshape(TT, P, SEQ).transpose(1, 0, 2).reshape(P, TT * SEQ)
    t["dft_c"], t["dft_s"] = tiled(np.cos(a)), tiled(np.sin(a))
    g = np.arange(64)
    a = 2 * np.pi * (np.outer(g, g) % 64) / 64
    scale = 1.0 / np.sqrt(SEQ * 64)
    t["group_c"] = np.kron(np.eye(2), np.cos(a)) * scale
    t["group_s"] = np.kron(np.eye(2), -np.sin(a)) * scale
    t["upper"] = np.triu(np.ones((P, P)))
    q, k = np.arange(P)[:, None], np.arange(SEQ)[None, :]
    dist = [np.where(q + P * i >= k, q + P * i - k, 1e32) for i in range(TT)]
    t["dist"] = np.concatenate(dist, axis=1)
    count = [np.minimum(n + w // 2, SEQ) - np.maximum(n - w // 2, 0) for w in WINDOWS]
    t["count"] = np.tile((1.0 / np.stack(count)).reshape(1, -1), (P, 1))
    rot_dim = DH3 // 4
    inv = (1.0 / (np.float32(500000.0) ** (np.arange(0, rot_dim, 2, dtype=np.float32) / np.float32(rot_dim)))).astype(np.float32)
    ang = (n.astype(np.float32)[:, None] * inv[None, :]).astype(np.float32).astype(np.float64)
    c64, s64, turn = np.ones((DH3, SEQ)), np.zeros((DH3, SEQ)), np.zeros((DH3, DH3))
    r = rot_dim // 2
    for i in range(r):
        c64[i] = c64[i + r] = np.cos(ang[:, i])
        s64[i] = s64[i + r] = np.sin(ang[:, i])
        turn[i, i + r], turn[i + r, i] = -1.0, 1.0
    t["cos3"], t["sin3"] = np.tile(c64, (2, 1)), np.tile(s64, (2, 1))
    t["turn3"] = np.kron(np.eye(2), turn).T
    for name, width in TABLES.items():
        assert t[name].shape == (P, width), (name, t[name].shape)
    return np.concatenate([t[name] for name in TABLES], axis=1).astype(np.float32)


LAYOUT = {
    "x": None, "ctx": None, "c": (P, KT), "c_ctx": (P, KT), "w_mod": (D, 6 * D), "b_mod": (48, P),
    "norm_attn_pre": (8, P), "norm_attn_post": (D,), "norm_ffn_pre": (8, P), "norm_ffn_post": (D,),
    "w_in": (D, W_IN1), "norm_q_lat": (3, P), "norm_kv_lat": (2, P), "w_q_up": (Q_RANK, 1152),
    "w_kv_up": (KV_RANK, 1536), "w_fourier": (4, 64, 64), "w_out": (D, D), "w_router": (D, E), "b_router": (E,),
    "w_gate": (E, D, DFF), "b_gate": (256, P), "w_up": (E, D, DFF), "b_up": (256, P), "w_down": (E, DFF, D),
    "b_down": (E, D), "w_in_2": (D, W2), "sg_w_2": (4, P, P), "sg_b_2": (512,), "v_ln_g_2": (D_A,),
    "v_ln_b_2": (D_A,), "conv_w_2": (124, P), "conv_b_2": (4, P), "cv_ln_g_2": (4, P), "cv_ln_b_2": (4, P),
    "w_branch_2": (3, 512, D), "w_out_2": (D, D), "ln_g_2": (D,), "ln_b_2": (D,), "c_3": (P, KT),
    "mod_w_3": (LAYERS, D, MODS3 * D), "mod_b_3": (144, P), "norm_g_3": (48, P),
    "ffn_w_gu_3": (LAYERS, 2, D, 2 * DFF3), "ffn_w_down_3": (LAYERS, 2, DFF3, D), "pool_w_3": (4, 256, 256),
    "pool_scale_3": (D,), "diff_w_qkv_3": (D, 3 * D), "diff_lambda_3": (256,), "diff_subln_g_3": (1, P),
    "diff_w_o_3": (D, D), "final_g_3": (D,),
}


def kernel(**inputs):
    import concourse.bacc as bacc
    from concourse.bass_utils import run_bass_kernel_spmd

    nc = bacc.Bacc("TRN2", target_bir_lowering=False, num_devices=1)
    arrays, ins = {}, {}

    def give(name, a):
        arrays[f"in_{name}"] = a
        return nc.dram_tensor(f"in_{name}", a.shape, F32, kind="ExternalInput").ap()

    for name, shape in LAYOUT.items():
        a = np.ascontiguousarray(inputs[name])
        if shape is None:
            ins[name] = give(name, a.reshape(SEQ, D)).rearrange("(t p) d -> p t d", p=P)
        else:
            ins[name] = give(name, a.reshape(shape))
    ins["b_mod_row"] = ins["b_mod"].rearrange("a b -> (a b)")
    ins["mod_b_3_row"] = ins["mod_b_3"].rearrange("a b -> (a b)")
    ins["tables"] = give("tables", tables())
    out = nc.dram_tensor("out", (SEQ, D), F32, kind="ExternalOutput").ap()
    program(nc, ins, out.rearrange("(t p) d -> p t d", p=P))
    result = run_bass_kernel_spmd(nc, [arrays], core_ids=[0])
    return result.results[0]["out"].reshape(1, SEQ, D)
```
